# Optimizing a Trainium2 kernel written in Bass

```python
import math
import jax
import jax.numpy as jnp
from jax import lax
import numpy as np

D_MODEL = 1024
BATCH = 1
SEQ = 256
DEPTH = 2

GRID_W = 64
CTX_LEN = 256
HEAD_DIM = 64
ROPE_THETA = 10000.0
NORM_EPS = 1e-6
NEG_INF = -1e30

A_HEADS = 4
A_KV_HEADS = 2
WINDOW = 128
A_BLOCK = 128
SSD_HEADS = 4
SSD_HEAD_DIM = 64
SSD_GROUPS = 2
SSD_STATE = 64
SSD_CHUNK = 128
SSD_CONV = 4
LRU_WIDTH = 256
LRU_BLOCKS = 4
LRU_BLOCK_DIM = LRU_WIDTH // LRU_BLOCKS
LRU_CONV = 4
LRU_C = 8.0
D_HEADS = 4
D_KV_HEADS = 2
Q_BLOCK = 128
N_EXPERTS = 64
N_EXPERT_GROUPS = 8
TOPK_GROUPS = 4
TOP_K = 8
EXPERT_HIDDEN = 256
SHARED_HIDDEN = 256
ROUTED_SCALE = 2.5
MOE_BLOCK = 128

A_Q = A_HEADS * HEAD_DIM
A_KV = A_KV_HEADS * HEAD_DIM
SSD_INNER = SSD_HEADS * SSD_HEAD_DIM
SSD_BC = SSD_GROUPS * SSD_STATE
SSD_CONV_CH = SSD_INNER + 2 * SSD_BC
D_Q = D_HEADS * HEAD_DIM
D_KV = D_KV_HEADS * HEAD_DIM
IN_SPLITS = (A_Q, A_KV, A_KV,
             SSD_INNER, SSD_INNER, SSD_BC, SSD_BC, SSD_HEADS, SSD_HEADS,
             LRU_WIDTH, LRU_WIDTH,
             D_Q, D_KV, D_KV)
IN_PROJ = sum(IN_SPLITS)
IN_CUTS = tuple(sum(IN_SPLITS[:i + 1]) for i in range(len(IN_SPLITS) - 1))
MIX_WIDTH = A_Q + SSD_INNER + LRU_WIDTH + D_Q

kernel_name = 'hybrid_diffusion_block'

def rms_norm(x, gain):
    xf = x.astype(jnp.float32)
    y = xf * lax.rsqrt(jnp.mean(xf * xf, axis=-1, keepdims=True) + NORM_EPS)
    return (y * gain.astype(jnp.float32)).astype(x.dtype)

def modulate(x, shift, scale):
    return x * (1 + scale) + shift

def split_heads(t):
    return t.reshape(t.shape[:-1] + (t.shape[-1] // HEAD_DIM, HEAD_DIM))

def seq_cat(u, v):
    return jnp.concatenate([u, v], axis=1)

def rev_cat(u, v):
    return jnp.concatenate([jnp.flip(u, 1), jnp.flip(v, 1)], axis=1)

def axial_rope_tables(n_rows):
    t = jnp.arange(n_rows * GRID_W)
    row = (t // GRID_W).astype(jnp.float32)
    col = (t % GRID_W).astype(jnp.float32)
    axis_dim = HEAD_DIM // 2
    inv_freq = ROPE_THETA ** (-jnp.arange(0, axis_dim, 2, dtype=jnp.float32) / axis_dim)
    ang = jnp.concatenate([row[:, None] * inv_freq, col[:, None] * inv_freq], axis=-1)
    return jnp.cos(ang), jnp.sin(ang)

def apply_rope(x, cos, sin):
    xf = x.astype(jnp.float32).reshape(x.shape[:-1] + (HEAD_DIM // 2, 2))
    x1, x2 = xf[..., 0], xf[..., 1]
    c = cos[None, :, None, :]
    s = sin[None, :, None, :]
    out = jnp.stack([x1 * c - x2 * s, x1 * s + x2 * c], axis=-1)
    return out.reshape(x.shape).astype(x.dtype)

def dense_gqa(q, k, v, sink=None):
    b, tq, hq, d = q.shape
    hkv = k.shape[2]
    grp = hq // hkv
    qg = q.reshape(b, tq, hkv, grp, d)
    s = jnp.einsum('bqhgd,bkhd->bhgqk', qg, k).astype(jnp.float32) * d ** -0.5
    if sink is not None:
        s_sink = jnp.broadcast_to(sink.astype(jnp.float32).reshape(1, hkv, grp, 1, 1), s.shape[:-1] + (1,))
        p = jax.nn.softmax(jnp.concatenate([s, s_sink], axis=-1), axis=-1)[..., :-1]
    else:
        p = jax.nn.softmax(s, axis=-1)
    o = jnp.einsum('bhgqk,bkhd->bqhgd', p.astype(v.dtype), v)
    return o.reshape(b, tq, hq * d)

def window_attention(q_l, k_l, v_l, q_c, k_c, v_c, sink, with_ctx):
    b, S, hq, d = q_l.shape
    hkv = k_l.shape[2]
    grp = hq // hkv
    nb = S // A_BLOCK
    n_ctx = k_c.shape[1]
    qb = q_l.reshape(b, nb, A_BLOCK, hkv, grp, d)

    def band(t):
        z = jnp.zeros((b, A_BLOCK) + t.shape[2:], t.dtype)
        tp = jnp.concatenate([z, t, z], axis=1).reshape((b, nb + 2, A_BLOCK) + t.shape[2:])
        return jnp.concatenate([tp[:, :-2], tp[:, 1:-1], tp[:, 2:]], axis=2)

    kb, vb = band(k_l), band(v_l)
    scale = d ** -0.5
    s_win = jnp.einsum('bnqhgd,bnkhd->bnhgqk', qb, kb).astype(jnp.float32) * scale
    q_off = jnp.arange(A_BLOCK)[:, None]
    k_off = jnp.arange(3 * A_BLOCK)[None, :] - A_BLOCK
    k_abs = jnp.arange(nb)[:, None, None] * A_BLOCK + k_off
    valid = (jnp.abs(k_off - q_off) <= WINDOW) & (k_abs >= 0) & (k_abs < S)
    s_win = jnp.where(valid[None, :, None, None], s_win, NEG_INF)
    s_ctx = jnp.einsum('bnqhgd,bkhd->bnhgqk', qb, k_c).astype(jnp.float32) * scale
    s_sink = jnp.broadcast_to(sink.astype(jnp.float32).reshape(1, 1, hkv, grp, 1, 1), s_win.shape[:-1] + (1,))
    p = jax.nn.softmax(jnp.concatenate([s_win, s_ctx, s_sink], axis=-1), axis=-1).astype(v_l.dtype)
    n_win = 3 * A_BLOCK
    o = (jnp.einsum('bnhgqk,bnkhd->bnqhgd', p[..., :n_win], vb)
         + jnp.einsum('bnhgqk,bkhd->bnqhgd', p[..., n_win:n_win + n_ctx], v_c))
    o_l = o.reshape(b, S, hq * d)
    o_c = dense_gqa(q_c, k_c, v_c, sink) if with_ctx else None
    return o_c, o_l

def global_attention(q_l, k_l, v_l, q_c, k_c, v_c, with_ctx):
    b, S, hq, d = q_l.shape
    nb = S // Q_BLOCK
    k_all = seq_cat(k_c, k_l)
    v_all = seq_cat(v_c, v_l)
    q_blocks = jnp.moveaxis(q_l.reshape(b, nb, Q_BLOCK, hq, d), 1, 0)
    o = lax.map(lambda qb: dense_gqa(qb, k_all, v_all), q_blocks)
    o_l = jnp.moveaxis(o, 0, 1).reshape(b, S, hq * d)
    o_c = dense_gqa(q_c, k_c, v_c) if with_ctx else None
    return o_c, o_l

def depthwise_conv(x, w, bias):
    width, ch = w.shape
    left = width // 2
    y = lax.conv_general_dilated(x, w[:, None, :], (1,), [(left, width - 1 - left)],
                                 dimension_numbers=('NWC', 'WIO', 'NWC'), feature_group_count=ch)
    return y + bias

def ssd_chunked_scan(x, dt, a_neg, bmat, cmat):
    b, T, h, p = x.shape
    n = bmat.shape[-1]
    nc = T // SSD_CHUNK
    xc = x.astype(jnp.float32).reshape(b, nc, SSD_CHUNK, h, p)
    bc = bmat.astype(jnp.float32).reshape(b, nc, SSD_CHUNK, h, n)
    cc = cmat.astype(jnp.float32).reshape(b, nc, SSD_CHUNK, h, n)
    dtc = dt.astype(jnp.float32).reshape(b, nc, SSD_CHUNK, h)
    a_cum = jnp.cumsum(dtc * a_neg, axis=2)
    seg = a_cum[:, :, :, None, :] - a_cum[:, :, None, :, :]
    lower = jnp.tril(jnp.ones((SSD_CHUNK, SSD_CHUNK), bool))
    decay = jnp.exp(jnp.where(lower[:, :, None], seg, -jnp.inf))
    w_ij = jnp.einsum('bcihn,bcjhn->bcijh', cc, bc) * decay * dtc[:, :, None]
    y_intra = jnp.einsum('bcijh,bcjhp->bcihp', w_ij, xc)
    to_end = jnp.exp(a_cum[:, :, -1:] - a_cum) * dtc
    states = jnp.einsum('bcjhn,bcjh,bcjhp->bchpn', bc, to_end, xc)
    chunk_decay = jnp.exp(a_cum[:, :, -1])

    def step(carry, inp):
        st, dec = inp
        return carry * dec[..., None, None] + st, carry

    _, start = lax.scan(step, jnp.zeros((b, h, p, n), jnp.float32),
                        (jnp.moveaxis(states, 1, 0), jnp.moveaxis(chunk_decay, 1, 0)))
    start = jnp.moveaxis(start, 0, 1)
    y_inter = jnp.einsum('bcihn,bchpn->bcihp', cc, start) * jnp.exp(a_cum)[..., None]
    return (y_intra + y_inter).reshape(b, T, h, p)

def ssd_mixer(parts_c, parts_l, conv_w, conv_b, dt_bias, a_log, d_skip, norm_gain, with_ctx):
    def prep(z, xs, bm, cm, dt_f, dt_b):
        b, t = xs.shape[:2]
        xbc = jax.nn.silu(depthwise_conv(jnp.concatenate([xs, bm, cm], axis=-1), conv_w, conv_b))
        xs, bm, cm = jnp.split(xbc, (SSD_INNER, SSD_INNER + SSD_BC), axis=-1)
        to_heads = lambda u: jnp.repeat(u.reshape(b, t, SSD_GROUPS, SSD_STATE), SSD_HEADS // SSD_GROUPS, axis=2)
        dt = jax.nn.softplus(jnp.stack([dt_f, dt_b]).astype(jnp.float32)
                             + dt_bias[:, None, None, :].astype(jnp.float32))
        return z, xs.reshape(b, t, SSD_HEADS, SSD_HEAD_DIM), to_heads(bm), to_heads(cm), dt

    z_c, x_c, b_c, c_c, dt_c = prep(*parts_c)
    z_l, x_l, b_l, c_l, dt_l = prep(*parts_l)
    n_ctx = x_c.shape[1]
    a_neg = -jnp.exp(a_log.astype(jnp.float32))
    y_f = ssd_chunked_scan(seq_cat(x_c, x_l), seq_cat(dt_c[0], dt_l[0]), a_neg[0],
                           seq_cat(b_c, b_l), seq_cat(c_c, c_l))
    y_b = ssd_chunked_scan(rev_cat(x_c, x_l), rev_cat(dt_c[1], dt_l[1]), a_neg[1],
                           rev_cat(b_c, b_l), rev_cat(c_c, c_l))

    def finish(y_fwd, y_bwd_rev, xs, z):
        y = (y_fwd + jnp.flip(y_bwd_rev, 1)).astype(xs.dtype) + xs * d_skip[:, None]
        y = y.reshape(y.shape[:2] + (SSD_INNER,))
        return rms_norm(y * jax.nn.silu(z), norm_gain)

    out_l = finish(y_f[:, n_ctx:], y_b[:, n_ctx:], x_l, z_l)
    out_c = finish(y_f[:, :n_ctx], y_b[:, :n_ctx], x_c, z_c) if with_ctx else None
    return out_c, out_l

def rglru_scan(u, w_a, b_a, w_i, b_i, lam):
    b, T, ch = u.shape
    uf = u.astype(jnp.float32)
    ub = uf.reshape(b, T, LRU_BLOCKS, LRU_BLOCK_DIM)

    def gate(w, bias):
        return jax.nn.sigmoid(jnp.einsum('btki,kij->btkj', ub, w.astype(jnp.float32)).reshape(b, T, ch)
                              + bias.astype(jnp.float32))

    r = gate(w_a, b_a)
    i = gate(w_i, b_i)
    log_a = -LRU_C * r * jax.nn.softplus(-lam.astype(jnp.float32))
    a = jnp.exp(log_a)
    inp = jnp.sqrt(-jnp.expm1(2.0 * log_a)) * (i * uf)

    def combine(left, right):
        a1, h1 = left
        a2, h2 = right
        return a1 * a2, a2 * h1 + h2

    _, hs = lax.associative_scan(combine, (a, inp), axis=1)
    return hs

def rglru_mixer(x_c, g_c, x_l, g_l, conv_w, conv_b, w_a, b_a, w_i, b_i, lam, with_ctx):
    u_c = depthwise_conv(x_c, conv_w, conv_b)
    u_l = depthwise_conv(x_l, conv_w, conv_b)
    n_ctx = u_c.shape[1]
    h_f = rglru_scan(seq_cat(u_c, u_l), w_a[0], b_a[0], w_i[0], b_i[0], lam[0])
    h_b = rglru_scan(rev_cat(u_c, u_l), w_a[1], b_a[1], w_i[1], b_i[1], lam[1])

    def finish(hf, hb_rev, g):
        return (hf + jnp.flip(hb_rev, 1)).astype(g.dtype) * jax.nn.gelu(g)

    out_l = finish(h_f[:, n_ctx:], h_b[:, n_ctx:], g_l)
    out_c = finish(h_f[:, :n_ctx], h_b[:, :n_ctx], g_c) if with_ctx else None
    return out_c, out_l

def token_mixing(x_c, x_l, mod_c, mod_l, rope_cos, rope_sin, g_pre, g_post, w_in, w_out,
                 a_sink, ssd_conv_w, ssd_conv_b, ssd_dt_bias, ssd_a_log, ssd_d, ssd_norm,
                 lru_conv_w, lru_conv_b, lru_w_a, lru_b_a, lru_w_i, lru_b_i, lru_lambda,
                 d_q_norm, d_k_norm, with_ctx):
    shift_c, scale_c, gate_c = mod_c
    shift_l, scale_l, gate_l = mod_l

    def project(x, shift, scale):
        h = modulate(rms_norm(x, g_pre), shift, scale)
        return jnp.split(h @ w_in, IN_CUTS, axis=-1)

    pc = project(x_c, shift_c, scale_c)
    pl = project(x_l, shift_l, scale_l)
    rope = lambda t: apply_rope(t, rope_cos, rope_sin)
    qk_norm = lambda t, g: rms_norm(split_heads(t), g)

    oa_c, oa_l = window_attention(rope(split_heads(pl[0])), rope(split_heads(pl[1])), split_heads(pl[2]),
                                  split_heads(pc[0]), split_heads(pc[1]), split_heads(pc[2]), a_sink, with_ctx)
    ob_c, ob_l = ssd_mixer(pc[3:9], pl[3:9], ssd_conv_w, ssd_conv_b, ssd_dt_bias, ssd_a_log, ssd_d, ssd_norm,
                           with_ctx)
    oc_c, oc_l = rglru_mixer(pc[9], pc[10], pl[9], pl[10], lru_conv_w, lru_conv_b, lru_w_a, lru_b_a,
                             lru_w_i, lru_b_i, lru_lambda, with_ctx)
    od_c, od_l = global_attention(rope(qk_norm(pl[11], d_q_norm)), rope(qk_norm(pl[12], d_k_norm)),
                                  split_heads(pl[13]), qk_norm(pc[11], d_q_norm), qk_norm(pc[12], d_k_norm),
                                  split_heads(pc[13]), with_ctx)

    def merge(x, outs, gate):
        return x + gate * rms_norm(jnp.concatenate(outs, axis=-1) @ w_out, g_post)

    x_l = merge(x_l, (oa_l, ob_l, oc_l, od_l), gate_l)
    if with_ctx:
        x_c = merge(x_c, (oa_c, ob_c, oc_c, od_c), gate_c)
    return x_c, x_l

def routed_experts(h, expert_idx, expert_w, w_gate, w_up, w_down):
    n_tok, d = h.shape
    n_assign = n_tok * TOP_K
    flat_e = expert_idx.reshape(-1)
    order = jnp.argsort(flat_e)
    e_sorted = flat_e[order]
    counts = jnp.bincount(flat_e, length=N_EXPERTS)
    padded = (counts + MOE_BLOCK - 1) // MOE_BLOCK * MOE_BLOCK
    start = jnp.cumsum(counts) - counts
    padded_end = jnp.cumsum(padded)
    dest = (padded_end - padded)[e_sorted] + jnp.arange(n_assign) - start[e_sorted]
    n_blocks = -(-n_assign // MOE_BLOCK) + N_EXPERTS
    n_slots = n_blocks * MOE_BLOCK
    slot_tok = jnp.zeros((n_slots,), jnp.int32).at[dest].set((order // TOP_K).astype(jnp.int32))
    slot_w = jnp.zeros((n_slots,), h.dtype).at[dest].set(expert_w.reshape(-1)[order].astype(h.dtype))
    block_e = jnp.minimum(jnp.searchsorted(padded_end, jnp.arange(n_blocks) * MOE_BLOCK, side='right'),
                          N_EXPERTS - 1)

    def run_block(args):
        tok, wt, e = args
        xb = h[tok]
        hid = jax.nn.silu(xb @ w_gate[e]) * (xb @ w_up[e])
        return (hid @ w_down[e]) * wt[:, None]

    y = lax.map(run_block, (slot_tok.reshape(n_blocks, MOE_BLOCK), slot_w.reshape(n_blocks, MOE_BLOCK), block_e))
    return jax.ops.segment_sum(y.reshape(n_slots, d), slot_tok, num_segments=n_tok)

def moe_ffn(h, router_w, router_bias, w_gate, w_up, w_down, sh_gate, sh_up, sh_down):
    n_tok = h.shape[0]
    scores = jax.nn.sigmoid((h @ router_w).astype(jnp.float32))
    biased = scores + router_bias.astype(jnp.float32)
    grouped = biased.reshape(n_tok, N_EXPERT_GROUPS, N_EXPERTS // N_EXPERT_GROUPS)
    group_score = jnp.sum(lax.top_k(grouped, 2)[0], axis=-1)
    _, top_groups = lax.top_k(group_score, TOPK_GROUPS)
    group_mask = jnp.sum(jax.nn.one_hot(top_groups, N_EXPERT_GROUPS, dtype=jnp.float32), axis=1) > 0
    expert_mask = jnp.repeat(group_mask, N_EXPERTS // N_EXPERT_GROUPS, axis=1)
    _, idx = lax.top_k(jnp.where(expert_mask, biased, -jnp.inf), TOP_K)
    w = jnp.take_along_axis(scores, idx, axis=1)
    w = w / jnp.sum(w, axis=-1, keepdims=True) * ROUTED_SCALE
    shared = (jax.nn.silu(h @ sh_gate) * (h @ sh_up)) @ sh_down
    return routed_experts(h, idx, w, w_gate, w_up, w_down) + shared

def channel_mixing(x_c, x_l, mod_c, mod_l, g_pre, g_post, router_w, router_bias, w_gate, w_up, w_down,
                   sh_gate, sh_up, sh_down, with_ctx):
    shift_c, scale_c, gate_c = mod_c
    shift_l, scale_l, gate_l = mod_l
    b, S, d = x_l.shape
    tokens = modulate(rms_norm(x_l, g_pre), shift_l, scale_l).reshape(b * S, d)
    if with_ctx:
        h_c = modulate(rms_norm(x_c, g_pre), shift_c, scale_c).reshape(-1, d)
        tokens = jnp.concatenate([h_c, tokens], axis=0)
    y = moe_ffn(tokens, router_w, router_bias, w_gate, w_up, w_down, sh_gate, sh_up, sh_down)
    n_c = tokens.shape[0] - b * S
    x_l = x_l + gate_l * rms_norm(y[n_c:].reshape(b, S, d), g_post)
    if with_ctx:
        x_c = x_c + gate_c * rms_norm(y[:n_c].reshape(x_c.shape), g_post)
    return x_c, x_l

def setup_inputs(seed: int = 0) -> dict:
    key = jax.random.key(seed)
    ks = iter(jax.random.split(key, 48))
    L = DEPTH
    f32 = jnp.float32

    def normal(shape, scale):
        return jax.random.normal(next(ks), shape, f32) * scale

    def gain(shape):
        return 1.0 + normal(shape, 0.05)

    def uniform(shape, lo, hi):
        return jax.random.uniform(next(ks), shape, f32, lo, hi)

    a_pow = uniform((L, 2, LRU_WIDTH), 0.9, 0.999) ** (1.0 / LRU_C)
    dt0 = jnp.exp(uniform((L, 2, SSD_HEADS), math.log(1e-3), math.log(1e-1)))
    return {
        'x': normal((BATCH, SEQ, D_MODEL), 1.0),
        'c': normal((BATCH, D_MODEL), 1.0),
        'ctx': normal((BATCH, CTX_LEN, D_MODEL), 1.0),
        'c_ctx': normal((D_MODEL,), 1.0),
        'w_ada': normal((L, D_MODEL, 6 * D_MODEL), 0.5 * D_MODEL ** -0.5),
        'b_ada': normal((L, 6 * D_MODEL), 0.02),
        'g_mix_pre': gain((L, D_MODEL)),
        'g_mix_post': gain((L, D_MODEL)),
        'g_ffn_pre': gain((L, D_MODEL)),
        'g_ffn_post': gain((L, D_MODEL)),
        'w_in': normal((L, D_MODEL, IN_PROJ), D_MODEL ** -0.5),
        'w_out': normal((L, MIX_WIDTH, D_MODEL), MIX_WIDTH ** -0.5),
        'a_sink': normal((L, A_HEADS), 0.5),
        'ssd_conv_w': normal((L, SSD_CONV, SSD_CONV_CH), SSD_CONV ** -0.5),
        'ssd_conv_b': normal((L, SSD_CONV_CH), 0.02),
        'ssd_dt_bias': dt0 + jnp.log(-jnp.expm1(-dt0)),
        'ssd_a_log': jnp.log(uniform((L, 2, SSD_HEADS), 1.0, 16.0)),
        'ssd_d': gain((L, SSD_HEADS)),
        'ssd_norm': gain((L, SSD_INNER)),
        'lru_conv_w': normal((L, LRU_CONV, LRU_WIDTH), LRU_CONV ** -0.5),
        'lru_conv_b': normal((L, LRU_WIDTH), 0.02),
        'lru_w_a': normal((L, 2, LRU_BLOCKS, LRU_BLOCK_DIM, LRU_BLOCK_DIM), LRU_BLOCK_DIM ** -0.5),
        'lru_b_a': normal((L, 2, LRU_WIDTH), 0.02),
        'lru_w_i': normal((L, 2, LRU_BLOCKS, LRU_BLOCK_DIM, LRU_BLOCK_DIM), LRU_BLOCK_DIM ** -0.5),
        'lru_b_i': normal((L, 2, LRU_WIDTH), 0.02),
        'lru_lambda': jnp.log(a_pow) - jnp.log1p(-a_pow),
        'd_q_norm': gain((L, HEAD_DIM)),
        'd_k_norm': gain((L, HEAD_DIM)),
        'router_w': normal((L, D_MODEL, N_EXPERTS), D_MODEL ** -0.5),
        'router_bias': normal((L, N_EXPERTS), 0.01),
        'exp_w_gate': normal((L, N_EXPERTS, D_MODEL, EXPERT_HIDDEN), D_MODEL ** -0.5),
        'exp_w_up': normal((L, N_EXPERTS, D_MODEL, EXPERT_HIDDEN), D_MODEL ** -0.5),
        'exp_w_down': normal((L, N_EXPERTS, EXPERT_HIDDEN, D_MODEL), EXPERT_HIDDEN ** -0.5),
        'sh_w_gate': normal((L, D_MODEL, SHARED_HIDDEN), D_MODEL ** -0.5),
        'sh_w_up': normal((L, D_MODEL, SHARED_HIDDEN), D_MODEL ** -0.5),
        'sh_w_down': normal((L, SHARED_HIDDEN, D_MODEL), SHARED_HIDDEN ** -0.5),
    }

def reference(x, c, ctx, c_ctx, w_ada, b_ada, g_mix_pre, g_mix_post, g_ffn_pre, g_ffn_post, w_in, w_out,
              a_sink, ssd_conv_w, ssd_conv_b, ssd_dt_bias, ssd_a_log, ssd_d, ssd_norm,
              lru_conv_w, lru_conv_b, lru_w_a, lru_b_a, lru_w_i, lru_b_i, lru_lambda,
              d_q_norm, d_k_norm, router_w, router_bias, exp_w_gate, exp_w_up, exp_w_down,
              sh_w_gate, sh_w_up, sh_w_down):
    b = x.shape[0]
    n_rows = x.shape[1] // GRID_W
    rope_cos, rope_sin = axial_rope_tables(n_rows)
    silu_c = jax.nn.silu(c)
    silu_cc = jax.nn.silu(c_ctx)
    x_c, x_l = ctx, x
    for l in range(DEPTH):
        with_ctx = l < DEPTH - 1
        mod_l = (silu_c @ w_ada[l] + b_ada[l]).reshape(b, 6, 1, D_MODEL).transpose(1, 0, 2, 3)
        mod_c = (silu_cc @ w_ada[l] + b_ada[l]).reshape(6, D_MODEL)
        x_c, x_l = token_mixing(x_c, x_l, mod_c[:3], mod_l[:3], rope_cos, rope_sin,
                                g_mix_pre[l], g_mix_post[l], w_in[l], w_out[l],
                                a_sink[l], ssd_conv_w[l], ssd_conv_b[l], ssd_dt_bias[l], ssd_a_log[l],
                                ssd_d[l], ssd_norm[l], lru_conv_w[l], lru_conv_b[l], lru_w_a[l], lru_b_a[l],
                                lru_w_i[l], lru_b_i[l], lru_lambda[l], d_q_norm[l], d_k_norm[l], with_ctx)
        x_c, x_l = channel_mixing(x_c, x_l, mod_c[3:], mod_l[3:], g_ffn_pre[l], g_ffn_post[l],
                                  router_w[l], router_bias[l], exp_w_gate[l], exp_w_up[l], exp_w_down[l],
                                  sh_w_gate[l], sh_w_up[l], sh_w_down[l], with_ctx)
    return x_l


_drawn_inputs = setup_inputs


def setup_inputs(seed=0):
    import zlib

    import numpy as np

    out = dict(_drawn_inputs(seed))
    spreads = {}
    factors = {'a_sink': 8.0,
     'ssd_conv_b': 3.66,
     'ssd_d': 3.406,
     'lru_b_a': 6.584,
     'lru_b_i': 8.0,
     'd_q_norm': 8.0,
     'd_k_norm': 7.798}
    for name, (base, spread) in spreads.items():
        noise = np.random.default_rng([zlib.crc32(name.encode()), seed]).standard_normal(out[name].shape)
        drawn = base * np.exp(spread * noise) if base else spread * noise
        out[name] = jnp.asarray(drawn.astype(out[name].dtype))
    for name, factor in factors.items():
        out[name] = (out[name] * factor).astype(out[name].dtype)
    return out
```

```python
from contextlib import ExitStack

import concourse.bass as bass
from concourse import mybir

F32 = mybir.dt.float32
BF16 = mybir.dt.bfloat16
I32 = mybir.dt.int32
U32 = mybir.dt.uint32
ALU = mybir.AluOpType
ACT = mybir.ActivationFunctionType
AX = mybir.AxisListType.X

P = 128
DM = 1024
SEQ = 256
CTX = 256
T = CTX + SEQ
NT = T // P
DEPTH = 2
EPS = 1e-6
HD = 64
NE = 64
TOPK = 8
HID = 256
SLOTS = 64
NG = 8
ROUTED_SCALE = 2.5
MARK = -3.0e38
NEG = -1.0e30
BIG_ROW = 1.0e6
LRU_C = 8.0
C_A, C_Z, C_XBC, C_DT, C_LRU, C_D = 0, 512, 768, 1280, 1288, 1800
MAXB = (T * TOPK + NE * (SLOTS - 1)) // SLOTS
TABN = 144
CONST = [("ident", 128), ("triU", 128), ("triL", 128), ("iota", 128), ("cos", 64), ("sin", 64),
         ("cols", 16), ("triS", 128), ("negL", 128), ("negU", 128)]
CW = sum(w for _, w in CONST)
COFF = {}
_o = 0
for _n, _w in CONST:
    COFF[_n] = _o
    _o += _w
CKEEP = COFF["triS"]


def build(nc, I, out):
    ctx = ExitStack()
    with ctx:
        arena = ctx.enter_context(nc.sbuf_tensor("arena", [P, 53200], F32))
        top = [0]

        def region(words):
            a = top[0]
            top[0] += words
            assert top[0] <= 53200, top[0]
            return a

        def at(off, *shape):
            n = 1
            for s in shape:
                n *= s
            v = arena[:, off:off + n]
            if len(shape) == 1:
                return v
            names = "abcd"[:len(shape)]
            return v.rearrange("p (" + " ".join(names) + ") -> p " + " ".join(names),
                               **{k: s for k, s in zip(names[1:], shape[1:])})

        def at16(off, *shape):
            n = 1
            for s in shape:
                n *= s
            v = arena[:, off:off + (n + 1) // 2].bitcast(BF16)
            if len(shape) == 1:
                return v
            names = "abcd"[:len(shape)]
            return v.rearrange("p (" + " ".join(names) + ") -> p " + " ".join(names),
                               **{k: s for k, s in zip(names[1:], shape[1:])})

        rX = region(4096)
        rH = region(4096)
        rHT = region(4096)
        rMOD = region(6144)
        rRING = region(3 * 6144)
        rPROJ = region(9284)
        rXC = region(2048)
        rXT = region(1536)
        rC = region(CKEEP)
        rPar = region(256 + 384 + 512 + 64 + 66 + 40)
        rSm = region(420)
        rB16 = region(64 * 5)
        rMisc = region(300)

        X = at(rX, NT, DM)
        H = at(rH, NT, DM)
        HT = at(rHT, 8, T)
        MT = at(rHT, 8, T)
        MOD = at(rMOD, 3, 2, DM)
        ring = [rRING + 6144 * k for k in range(3)]
        QKV = {"A": at(rPROJ, NT, 512), "D": at(rPROJ + 2048, NT, 512)}
        Z = at(rPROJ + 4096, NT, 264)
        XBC = at(rPROJ + 5152, 4, 2, 259)
        LX = at(rPROJ + 7224, 2, 2, 259)
        LG = at(rPROJ + 8260, 2, T)
        XC = at(rXC, 4, T)
        XT = at(rXT, NT, 384)
        RAD1 = at(rXC, 4, P)
        RAD2 = at(rH + 3072, 1024)
        BD = at(rXT, 8, P)
        M64, B64, G64 = (at(rMOD + 5632 + P * k, P) for k in range(3))
        LR = [at(rMOD + 2048 * d, 2, T) for d in range(2)]
        LI = [at(rMOD + 2048 * d + 1024, 2, T) for d in range(2)]
        U = at(rH, 2, T)
        LT = [at(rH + 1024 + 1024 * d, 2, T) for d in range(2)]
        LD = at(rH + 3072, 2, T)
        XS = at(rPROJ + 5152, 2, NT, 256)
        ES = at(rPROJ + 5152, 2, 4, P)
        WS = at(rPROJ + 5152 + 1024, 2, 4, P)
        ST = at(rPROJ + 7224, 2, NT, P)
        YT = [at(rMOD + 256 * k, 256) for k in range(4)]
        YTD = at(rMOD + 256, 2, 4, 64)
        GATE_TMP = rMOD + 4096
        SQ = at(GATE_TMP, NT, 384)
        RT = [at(GATE_TMP + 384 * k, 2, 6, 32) for k in range(2)]
        QT = {"A": at(rH, 3, T), "D": at(rH + 1536, 3, T)}
        PB = [at(rPROJ + 5152 + 512 * k, 512) for k in range(3)]
        PTB = [at(rPROJ + 5152 + 1536 + 512 * k, 512) for k in range(2)]
        JUNK = at(rXC, DM)
        OTMP = [at(rXC + 1024 + 512 * k, 512) for k in range(2)]
        IDENT = at(rC + COFF["ident"], P)
        TRIU = at(rC + COFF["triU"], P)
        TRIL = at(rC + COFF["triL"], P)
        IOTA = at(rC + COFF["iota"], P)
        COS = at(rC + COFF["cos"], 2, 32)
        SIN = at(rC + COFF["sin"], 2, 32)
        COLS = at(rC + COFF["cols"], 16)
        CRAW = at(rH, 3, P)
        IDB, NEGL, NEGU, TRISB, ONESB = (at16(rB16 + 64 * k, P) for k in range(5))
        o = rPar
        SSDN = at(o, 256); o += 256
        GQK = at(o, 6, HD); o += 384
        RW = at(o, 8, NE); o += 512
        RB = at(o, NE); o += 64
        PC = at(o, 66); o += 66
        DTB = at(o, 8); o += 8
        ALOG = at(o, 8); o += 8
        DSK = at(o, 4); o += 4
        SINK = at(o, 4); o += 4
        NSINK = at(o, 4); o += 4
        CM = at(o, 4); o += 4
        PR = at(rMisc, P)
        o = rSm
        SS = at(o, 4); o += 4
        SSTD = at(o, 4); o += 4
        RSTD = at(o, 4); o += 4
        S8 = at(o, 8); o += 8
        V36, E36, D36, Z36, Q36, P36 = (at(o + 36 * k, 36) for k in range(6)); o += 216
        AA = at(o, NT, 8); o += 32
        STT8 = at(o, 24); o += 24
        STT9 = at(o, 24); o += 24
        MC = at(o, 16, 2); o += 32
        C8 = at(o, 4); o += 4
        NC8 = at(o, 4); o += 4
        EAL = at(o, 8); o += 8
        o = rMisc
        CT = at(o + 128, 96)
        DEC2 = at(o, NT, 2, 2)
        TOE = at(o + 16, NT, 8)
        NCUM = at(o + 48, 32)
        SCOL = at(o + 224, 3, 4)
        MX = at(o + 236, 3, 4)
        CT2 = CT
        HC = at(rMisc + 256, 2, 8)
        SILC = at(rMisc + 272, 8, 2)
        YS = at(rPROJ, NT, DM)
        o = rPROJ + 4096
        SC = at(o, NT, NE); o += 256
        BI = at(o, NT, NE); o += 256
        SEL = at(o, NT, NE); o += 256
        TOP = at(o, NT, NG, 8); o += 256
        MR = at(o, NT, NE); o += 256
        CI = at(o, NT, NE); o += 256
        GG = at(o, NT, NE); o += 256
        KV = at16(o, NT, NE, 3); o += 384
        SELB = at16(o, NT, NE); o += 128
        WK = at(o, NT, TOPK); o += 32
        GS12 = at(o, NT, 12); o += 48
        GR = at(o, NT, 12); o += 48
        M8 = at(o, NT, 8); o += 32
        CNT = at(o, NE); o += 64
        NB = at(o, NE); o += 64
        PEND = at(o, NE); o += 64
        PST = at(o, NE); o += 64
        LE = at(o, NE); o += 64
        RROW = at(o, P); o += 128
        WSUM = at(o, NT); o += 4
        EB = at(o, 4); o += 4
        OH = [at16(o + 256 * k, NT, P) for k in range(2)]; o += 512
        XG = [at(o + 512 * k, 512) for k in range(2)]; o += 1024
        HS = at(o, 256); o += 256
        assert o <= rPROJ + 9284, o - rPROJ
        HIDB = at(rMisc, 256)
        o = rXC
        XGT = [at(o + 512 * k, 4, 2, SLOTS) for k in range(2)]; o += 1024
        YSB = [at(o + 512 * k, 512) for k in range(2)]; o += 1024
        o = rXT
        HIDT = [at(o + 128 * k, 2, SLOTS) for k in range(2)]; o += 256
        SIXT = arena[:, o:o + TABN].bitcast(U32); o += TABN
        SIXS = [arena[:, o + k:o + k + 1].bitcast(U32) for k in range(2)]; o += 2
        GIX = [arena[:, o + k:o + k + 1].bitcast(U32) for k in range(2)]; o += 2
        TAB = arena[0:1, o:o + TABN].bitcast(I32); o += TABN
        TABP = arena[0:1, o:o + NE].bitcast(I32); o += NE
        NPR = arena[0:1, o:o + 1].bitcast(I32); o += 1
        NBH = at(o, 1); o += 1
        RR = at(o, 4); o += 4
        BASE = at(o, 1); o += 1
        M3 = at(o, 4); o += 4
        TK = at(o, 4); o += 4
        ONES64 = at(o, NE); o += 64
        SHT = at(rMOD, 2, T)
        SHS = at(rMOD + 1024, T)
        SGT = at(rMOD + 1536, T)
        assert o <= rXT + 1536
        YK = [at(rRING + 8192 * k, TOPK, DM) for k in range(2)]

        bank = [ctx.enter_context(nc.psum_tensor(f"bank{k}", [P, 512], F32)) for k in range(8)]

        mod_raw = nc.dram_tensor("mod_raw", (2, 4 * DM), F32, kind="Internal").ap()
        mod_fin = nc.dram_tensor("mod_fin", (64, P), F32, kind="Internal").ap()
        hrows = nc.dram_tensor("hrows", (2 * (T + 1), 512), F32, kind="Internal").ap()
        yrows = nc.dram_tensor("yrows", (2 * (TOPK * T + 1), 512), F32, kind="Internal").ap()

        sems = []

        def sem(name):
            s = ctx.enter_context(nc.semaphore(name))
            sems.append(s)
            return s

        sp_land = [sem(f"sp_land{k}") for k in range(3)]
        sp_yk = [sem("sp_yk0"), sem("sp_yk1")]
        sp_go = sem("sp_go")
        act_par = sem("act_par")
        act_parm = sem("act_parm")
        act_pr = sem("act_pr")
        pool_clr = sem("pool_clr")
        pool_raw = sem("pool_raw")
        pool_m64 = sem("pool_m64")
        pool_fin = sem("pool_fin")
        pool_mod2 = sem("pool_mod2")
        pool_gate1 = sem("pool_gate1")
        pool_gate2 = sem("pool_gate2")
        pool_sq = sem("pool_sq")
        pool_nm = sem("pool_nm")
        pool_rope = sem("pool_rope")
        pool_c = sem("pool_c")
        pool_hr = sem("pool_hr")
        pool_g = [sem("pool_g0"), sem("pool_g1")]
        pool_s = [sem("pool_s0"), sem("pool_s1")]
        pool_go = sem("pool_go")
        pe_piece = sem("pe_piece")
        pe_pc = sem("pe_pc")
        pe_m1 = sem("pe_m1")
        pe_tr = sem("pe_tr")
        pe_pj = sem("pe_pj")
        pe_lg = sem("pe_lg")
        pe_cum = sem("pe_cum")
        pe_xt = sem("pe_xt")
        pe_st = sem("pe_st")
        pe_cb = sem("pe_cb")
        pe_gt = sem("pe_gt")
        pe_in = sem("pe_in")
        pe_y = sem("pe_y")
        pe_ym = sem("pe_ym")
        pe_qk = sem("pe_qk")
        pe_s = sem("pe_s")
        pe_pt = sem("pe_pt")
        pe_o = sem("pe_o")
        pe_op = sem("pe_op")
        pe_rt = sem("pe_rt")
        pe_rtt = sem("pe_rtt")
        pe_sh = sem("pe_sh")
        pe_sd = sem("pe_sd")
        pe_rk = sem("pe_rk")
        pe_row = sem("pe_row")
        pe_meta = sem("pe_meta")
        pe_gu = sem("pe_gu")
        pe_dn = sem("pe_dn")
        pe_x = sem("pe_x")
        pe_h = sem("pe_h")
        pe_pv = sem("pe_pv")
        a_ss = sem("a_ss")
        a_tr = sem("a_tr")
        a_pj = sem("a_pj")
        a_ex36 = sem("a_ex36")
        a_al = sem("a_al")
        a_lg = sem("a_lg")
        a_lt = sem("a_lt")
        a_la = sem("a_la")
        a_lq = sem("a_lq")
        a_xc = sem("a_xc")
        a_z = sem("a_z")
        a_cum = sem("a_cum")
        a_xt = sem("a_xt")
        a_e = sem("a_e")
        a_ssy = sem("a_ssy")
        a_ym = sem("a_ym")
        a_qn = sem("a_qn")
        a_qk = sem("a_qk")
        a_ex = sem("a_ex")
        a_es = sem("a_es")
        a_pt = sem("a_pt")
        a_so = sem("a_so")
        a_rt = sem("a_rt")
        a_sh = sem("a_sh")
        a_sd = sem("a_sd")
        a_xe = sem("a_xe")
        a_si = sem("a_si")
        a_h = sem("a_h")
        a_y = sem("a_y")
        a_fs = sem("a_fs")
        v_q = sem("v_q")
        v_ada = sem("v_ada")
        v_m64 = sem("v_m64")
        v_pc = sem("v_pc")
        v_pcl = sem("v_pcl")
        v_h = sem("v_h")
        v_hm = sem("v_hm")
        v_v36 = sem("v_v36")
        v_c8 = sem("v_c8")
        v_u = sem("v_u")
        v_ld = sem("v_ld")
        v_lru = sem("v_lru")
        v_cv = sem("v_cv")
        v_aa = sem("v_aa")
        v_cum = sem("v_cum")
        v_xs = sem("v_xs")
        v_st = sem("v_st")
        v_w = sem("v_w")
        v_y = sem("v_y")
        v_yz = sem("v_yz")
        v_yn = sem("v_yn")
        v_qs = sem("v_qs")
        v_qr = sem("v_qr")
        v_nm = sem("v_nm")
        v_p = sem("v_p")
        v_ot = sem("v_ot")
        v_so = sem("v_so")
        v_x = sem("v_x")
        v_sc = sem("v_sc")
        v_shm = sem("v_shm")
        v_sel = sem("v_sel")
        v_eb = sem("v_eb")
        v_tab = sem("v_tab")
        v_oh = sem("v_oh")
        v_ix = sem("v_ix")
        v_hid = sem("v_hid")
        v_six = sem("v_six")
        v_ml = sem("v_ml")
        v_yk = sem("v_yk")
        v_ys = sem("v_ys")
        v_fs = sem("v_fs")
        v_end = sem("v_end")
        nums = [s.num for s in sems]
        assert nums == list(range(nums[0], nums[0] + len(nums)))
        all_sems = range(nums[0], nums[-1] + 1)

        N_ADA1, N_PROJ, N_ADA2 = 4, 5, 6
        N_ADA = N_ADA1 + N_ADA2
        P_PROJ, P_ADA2 = N_ADA1, N_ADA1 + N_PROJ
        P_OUT = P_ADA2 + N_ADA2
        P_SH = P_OUT + 2
        N_STATIC = P_SH + 1
        ada2_width = [768] * 5 + [256]

        def slot_of(n):
            return n % 3

        dmas_of = [1] * N_ADA1 + [2, 1, 1, 1, 1] + [1] * N_ADA2 + [1, 1] + [3]

        def landed(n):
            k = slot_of(n)
            return sp_land[k], 16 * sum(d for m, d in enumerate(dmas_of[:n + 1]) if slot_of(m) == k)

        base_land = [16 * sum(d for m, d in enumerate(dmas_of) if slot_of(m) == k) for k in range(3)]
        done_of = [(pe_piece, n + 1) for n in range(N_ADA1)] + [(pe_pj, 4 * k) for k in range(1, 6)]
        done_of += [(pe_piece, n + 1) for n in range(N_ADA1, N_ADA)] + [(pe_op, 8), (pe_op, 8), (pe_sd, 8)]

        with nc.Block() as block:
            @block.sync
            def _(sp):
                for t in range(2):
                    sp.dma_start(X[:, t, :], I["ctx"][0, t * P:(t + 1) * P, :]).then_inc(sp_land[0], 16)
                    sp.dma_start(X[:, 2 + t, :], I["x"][0, t * P:(t + 1) * P, :]).then_inc(sp_land[0], 16)
                sp.dma_start(at(rC, CKEEP), I["consts"][:, 0:CKEEP]).then_inc(sp_land[1], 16)
                sp.dma_start(CRAW, I["consts"][:, CKEEP:CW].rearrange("p (a b) -> p a b", a=3)).then_inc(sp_land[1], 16)
                sp.dma_start(HC[:, 0, :], I["c_ctx"].rearrange("(p c) -> p c", c=8)).then_inc(sp_land[2], 16)
                sp.dma_start(HC[:, 1, :], I["c"][0].rearrange("(p c) -> p c", c=8)).then_inc(sp_land[2], 16)
                sp.wait_ge(sp_land[0], 64)

            @block.scalar
            def _(act):
                act.wait_ge(sp_land[2], 32)
                act.activation(SILC, HC.rearrange("p s c -> p c s"), ACT.Silu).then_inc(a_z, 1)
                act.wait_ge(a_z, 1)

            @block.vector
            def _(dve):
                dve.wait_ge(sp_land[1], 32)
                dve.tensor_copy(IDB, IDENT).then_inc(v_q, 1)
                dve.tensor_copy(TRISB, CRAW[:, 0, :]).then_inc(v_q, 1)
                dve.tensor_copy(NEGL, CRAW[:, 1, :]).then_inc(v_q, 1)
                dve.tensor_copy(NEGU, CRAW[:, 2, :]).then_inc(v_q, 1)
                dve.memset(ONESB, 1.0).then_inc(v_q, 1)
                dve.memset(CM, 1.0).then_inc(v_q, 1)
                dve.wait_ge(v_q, 6)
        nc.all_engine_barrier(sems_to_clear=all_sems)

        def tile_of(t):
            return slice(t * P, (t + 1) * P)

        def lay(name, l):
            ap = I[name]
            rest = "bcdef"[:len(ap.shape) - 1]
            return ap[bass.ds(l, 1)].rearrange("a " + " ".join(rest) + " -> (a " + rest[0] + ") " + " ".join(rest[1:]))

        def row_bcast(ap):
            return ap.partition_broadcast(P)

        units = [(g, t, h) for g in "AD" for t in (2, 3, 0, 1) for h in range(4)]
        NU = len(units)
        score_bank = (0, 1, 6)

        def keys_of(t):
            return T if t >= 2 else CTX

        ringv = arena[:, rRING:rRING + 3 * 6144].rearrange("p (s w) -> p s w", s=3)

        with nc.Fori(0, DEPTH) as l:
          with nc.Block() as block:

            @block.sync
            def _(sp):
                w_in = lay("w_in", l).rearrange("(c p) n -> p c n", c=8)
                w_ada = lay("w_ada", l).rearrange("(p c) n -> p c n", c=8)
                w_out = lay("w_out", l).rearrange("(c p) n -> p c n", c=8)
                for n in range(N_STATIC):
                    k = slot_of(n)
                    if n >= 3:
                        sp.wait_ge(*done_of[n - 3])
                    if n < P_PROJ:
                        sp.dma_start(at(ring[k], 8, 512), w_ada[:, :, n * 512:(n + 1) * 512]).then_inc(sp_land[k], 16)
                    elif n == P_PROJ:
                        sp.dma_start(at(ring[k], 8, 264)[:, :, 0:256], w_in[:, :, C_Z:C_Z + 256]).then_inc(sp_land[k], 16)
                        sp.dma_start(at(ring[k], 8, 264)[:, :, 256:264], w_in[:, :, C_DT:C_DT + 8]).then_inc(sp_land[k], 16)
                    elif n < P_ADA2:
                        c0 = (C_LRU, C_XBC, C_A, C_D)[n - P_PROJ - 1]
                        sp.dma_start(at(ring[k], 8, 512), w_in[:, :, c0:c0 + 512]).then_inc(sp_land[k], 16)
                    elif n < P_OUT:
                        w, c0 = ada2_width[n - P_ADA2], 2 * DM + 768 * (n - P_ADA2)
                        sp.dma_start(at(ring[k], 8, w), w_ada[:, :, c0:c0 + w]).then_inc(sp_land[k], 16)
                    elif n < P_SH:
                        sp.dma_start(at(ring[k], 8, 512), w_out[:, :, (n - P_OUT) * 512:(n - P_OUT + 1) * 512]).then_inc(sp_land[k], 16)
                    else:
                        w = at(ring[k], 2, 8, HID)
                        sp.dma_start(w[:, 0], lay("sh_w_gate", l).rearrange("(p c) n -> p c n", c=8)).then_inc(sp_land[k], 16)
                        sp.dma_start(w[:, 1], lay("sh_w_up", l).rearrange("(p c) n -> p c n", c=8)).then_inc(sp_land[k], 16)
                        sp.dma_start(at(ring[k] + 4096, 2, DM), lay("sh_w_down", l).rearrange("(c p) n -> p c n", c=2)).then_inc(sp_land[k], 16)

                eg = I["exp_w_gate"].rearrange("l e k n -> (l e) k n")
                eu = I["exp_w_up"].rearrange("l e k n -> (l e) k n")
                ed = I["exp_w_down"].rearrange("l e k n -> (l e) k n")

                def load_up(e, k):
                    w = at(ring[k], 2, 2, 4, HID)
                    for j, src in enumerate((eg, eu)):
                        sp.dma_start(w[:, j].rearrange("p h c n -> p h (c n)"),
                                     src[bass.ds(l * NE + e, 1)].rearrange("a (h p c) n -> p (a h) (c n)", h=2, c=4)
                                     ).then_inc(sp_land[k], 16)

                def load_down(e, k):
                    sp.dma_start(at(ring[k] + 4096, 2 * DM),
                                 ed[bass.ds(l * NE + e, 1)].rearrange("a (p c) n -> p (a c n)", c=2)).then_inc(sp_land[k], 16)

                def reload(i, u):
                    used = sp.value_load(TABP[0:1, bass.ds(i * 3 + u, 1)], min_val=0, max_val=MAXB)
                    sp.wait_ge(sp_land[u], i * 48 + (base_land[u] + 48))
                    sp.sem_inc(sp_go, 1)
                    sp.wait_ge(pe_gu, used + 1)
                    sp.sem_inc(sp_go, 1)
                    load_up(i * 3 + (3 + u), u)
                    sp.wait_ge(pe_dn, used + 1)
                    sp.sem_inc(sp_go, 1)
                    load_down(i * 3 + (3 + u), u)

                for e in range(3):
                    sp.wait_ge(*done_of[P_OUT + e])
                    load_up(e, e)
                    load_down(e, e)
                sp.wait_ge(v_tab, 1)
                with sp.Fori(0, (NE - 4) // 3) as i:
                    for u in range(3):
                        reload(i, u)
                reload((NE - 4) // 3, 0)
                for k in range(3):
                    sp.wait_ge(sp_land[k], base_land[k] + 48 * ((NE - 1 - k) // 3 + 1))
                pairs = sp.value_load(NPR[0:1, 0:1], min_val=1, max_val=MAXB // 2 + 1)
                for u in range(2):
                    sp.wait_ge(pool_s[u], pairs * 16 + 16)
                sp.wait_ge(pe_dn, pairs * 2 + 1)
                sp.sem_inc(sp_go, 1)
                sp.wait_ge(pe_gu, pairs * 2 + 2)
                ysrc = yrows[2:2 * (TOPK * T + 1), :].rearrange("(k t p h) n -> t p k (h n)", k=TOPK, t=NT, h=2)
                for t in range(NT):
                    if t >= 2:
                        sp.wait_ge(v_yk, t - 1)
                    sp.dma_start(YK[t % 2], ysrc[t]).then_inc(sp_yk[t % 2], 16)

            @block.gpsimd
            def _(pool):
                pool.memset(RAD1, 0.0).then_inc(pool_clr, 1)
                pool.memset(at(rXT, 1024), 0.0).then_inc(pool_clr, 1)
                pool.memset(G64, 1.0).then_inc(pool_clr, 1)
                pool.memset(XBC[:, :, :, 0:2], 0.0).then_inc(pool_clr, 1)
                pool.memset(XBC[:, :, :, 258:259], 0.0).then_inc(pool_clr, 1)
                pool.memset(LX[:, :, :, 0:2], 0.0).then_inc(pool_clr, 1)
                pool.memset(LX[:, :, :, 258:259], 0.0).then_inc(pool_clr, 1)
                count = [0]

                def link(ins):
                    count[0] += 1
                    ins.then_inc(pool_c, 1)
                    pool.wait_ge(pool_c, count[0])

                def rope(g):
                    v = QKV[g][:, 2:4, 0:384].rearrange("p t (h d two) -> p t h d two", d=32, two=2)
                    x1, x2 = v[:, :, :, :, 0], v[:, :, :, :, 1]
                    cos = COS.unsqueeze(2).broadcast_to([P, 2, 6, 32])
                    sin = SIN.unsqueeze(2).broadcast_to([P, 2, 6, 32])
                    pool.tensor_tensor(RT[0], x1, cos, ALU.mult).then_inc(pool_c, 1)
                    count[0] += 1
                    link(pool.tensor_tensor(RT[1], x2, sin, ALU.mult))
                    link(pool.tensor_tensor(RT[0], RT[0], RT[1], ALU.subtract))
                    link(pool.tensor_tensor(RT[1], x1, sin, ALU.mult))
                    link(pool.tensor_tensor(x2, x2, cos, ALU.mult))
                    link(pool.tensor_tensor(x2, x2, RT[1], ALU.add))
                    pool.tensor_copy(x1, RT[0]).then_inc(pool_rope, 1)

                pool.wait_ge(a_pj, 16)
                rope("A")
                pool.wait_ge(pool_rope, 1)
                pool.wait_ge(a_pj, 20)
                qk = QKV["D"][:, :, 0:384]
                pool.tensor_tensor(SQ, qk, qk, ALU.mult).then_inc(pool_sq, 1)
                pool.wait_ge(v_qr, 1)
                qk4 = qk.rearrange("p t (h d) -> p t h d", d=HD)
                link(pool.tensor_tensor(qk4, qk4, STT8.rearrange("p (t h) -> p t h", h=6).unsqueeze(3)
                                        .broadcast_to([P, NT, 6, HD]), ALU.mult))
                pool.wait_ge(act_par, PARAMS)
                link(pool.tensor_tensor(qk4, qk4, GQK.unsqueeze(1).broadcast_to([P, NT, 6, HD]), ALU.mult))
                rope("D")
                pool.wait_ge(pool_rope, 2)
                pool.wait_ge(v_ada, N_ADA)
                raw = mod_raw[:, 0:3840].rearrange("s (n j w) -> j s n w", n=5, j=4)
                raw_end = mod_raw[:, 3840:4096].rearrange("s (j w) -> j s w", j=4)
                for j in range(4):
                    rows = RAD2[32 * j:32 * j + 2]
                    pool.dma_start(raw[j], rows[:, 0:960].rearrange("s (n w) -> s n w", n=5)).then_inc(pool_raw, 16)
                    pool.dma_start(raw_end[j], rows[:, 960:1024]).then_inc(pool_raw, 16)
                pool.wait_ge(pool_raw, 128)
                pool.dma_start(M64[0:64, :], mod_raw.rearrange("s (m p) -> (s m) p", p=P)).then_inc(pool_m64, 16)
                pool.wait_ge(v_m64, 1)
                pool.dma_start(mod_fin, M64[0:64, :]).then_inc(pool_fin, 16)
                pool.wait_ge(pool_fin, 16)
                fin = mod_fin.rearrange("(s m k) p -> m s (k p)", s=2, m=4)
                pool.dma_start(MOD[:, 2], row_bcast(fin[0])).then_inc(pool_gate1, 16)
                pool.wait_ge(v_yn, 4)
                pool.wait_ge(v_lru, 1)
                pool.dma_start(MOD[:, 0], row_bcast(fin[2])).then_inc(pool_mod2, 16)
                pool.dma_start(MOD[:, 1], row_bcast(fin[1])).then_inc(pool_mod2, 16)
                pool.wait_ge(v_x, 4)
                pool.dma_start(MOD[:, 2], row_bcast(fin[3])).then_inc(pool_gate2, 16)
                for k in range(2):
                    pool.memset(XG[k], 0.0).then_inc(pool_clr, 1)
                pool.wait_ge(pool_clr, 9)
                hdst = hrows[2:2 * (T + 1), :].rearrange("(t p h) n -> t p (h n)", t=NT, h=2)
                for t in range(NT):
                    pool.wait_ge(v_h, NT + t + 1)
                    pool.dma_start(hdst[t], H[:, t, :]).then_inc(pool_hr, 16)
                pool.wait_ge(pool_hr, 64)
                for k in range(2):
                    pool.dma_start(hrows[k:k + 1, :], X[0:1, 0, 0:512]).then_inc(pool_s[k], 16)

                def gather(k):
                    pool.indirect_dma_start(out=XG[k], out_offset=None, in_=hrows,
                                            in_offset=bass.IndirectOffsetOnAxis(ap=GIX[k], axis=0),
                                            bounds_check=2 * (T + 1) - 1, oob_is_err=False).then_inc(pool_g[k], 16)

                for b in range(3):
                    pool.wait_ge(v_ix, b + 1)
                    if b >= 2:
                        pool.wait_ge(pe_x, b - 1)
                    gather(b % 2)
                pairs = pool.value_load(NPR[0:1, 0:1], min_val=1, max_val=MAXB // 2 + 1)
                with pool.Fori(0, pairs) as i:
                    for u in range(2):
                        pool.wait_ge(v_ix, i * 2 + (u + 4))
                        pool.wait_ge(pe_x, i * 2 + (u + 2))
                        pool.sem_inc(pool_go, 1)
                        gather((u + 1) % 2)
                        pool.wait_ge(v_six, i * 2 + (u + 1))
                        pool.wait_ge(a_y, i * 2 + (u + 3))
                        pool.sem_inc(pool_go, 1)
                        pool.indirect_dma_start(out=yrows, out_offset=bass.IndirectOffsetOnAxis(ap=SIXS[u], axis=0),
                                                in_=YSB[u], in_offset=None,
                                                bounds_check=2 * (TOPK * T + 1) - 1, oob_is_err=False
                                                ).then_inc(pool_s[u], 16)
                pool.wait_ge(pool_g[0], pairs * 16 + 32)
                pool.wait_ge(pool_g[1], pairs * 16 + 16)
                for u in range(2):
                    pool.wait_ge(pool_s[u], pairs * 16 + 16)
                pool.sem_inc(pool_go, 1)
                pool.dma_reset(all_sems)

            @block.scalar
            def _(act):
                EPSC = COLS[:, 4:5]

                def norm_stats(base, waits):
                    for t in range(NT):
                        if waits:
                            act.wait_ge(v_x, t + 1)
                        if t:
                            act.wait_ge(a_ss, base + t)
                        act.activation(H[:, 0, :], X[:, t, :], ACT.Square, accum_out=SS[:, t:t + 1]).then_inc(a_ss, 1)
                    act.wait_ge(a_ss, base + 4)
                    act.activation(SSTD, SS, ACT.Sqrt, bias=EPSC, scale=1.0 / DM).then_inc(a_ss, 1)

                def out_of_transposes(base):
                    for j in range(8):
                        act.wait_ge(pe_tr, base + j + 1)
                        t, hh = j // 2, j % 2
                        act.activation(HT[:, 4 * hh:4 * hh + 4, tile_of(t)],
                                       bank[6 + j % 2][:, :].rearrange("p (c n) -> p c n", c=4), ACT.Copy).then_inc(a_tr, 1)

                norm_stats(0, False)
                r = 0
                for name, rows, pat in (("lru_conv_w", 8, "j (k p) -> (j k) p"), ("lru_conv_b", 2, "(k p) -> k p"),
                                        ("lru_b_a", 4, "d (k p) -> (d k) p"), ("lru_b_i", 4, "d (k p) -> (d k) p"),
                                        ("lru_lambda", 4, "d (k p) -> (d k) p"), ("ssd_conv_w", 16, "j (k p) -> (j k) p"),
                                        ("ssd_conv_b", 4, "(k p) -> k p"), ("b_ada", 16, "(m p) -> m p"),
                                        ("g_mix_pre", 8, "(m p) -> m p")):
                    act.dma_start(PR[r:r + rows, :], lay(name, l).rearrange(pat, p=P)[0:rows]).then_inc(act_pr, 16)
                    r += rows
                out_of_transposes(0)
                n = 0
                act.wait_ge(pool_clr, 3)
                for s in range(2):
                    act.dma_start(B64[32 * s:32 * s + 32, :], lay("b_ada", l).rearrange("(m p) -> m p", p=P)[16:48]).then_inc(act_parm, 16)
                    for m, name in ((0, "g_mix_post"), (2, "g_ffn_pre"), (3, "g_ffn_post")):
                        r = 32 * s + 8 * m
                        act.dma_start(G64[r:r + 8, :], lay(name, l).rearrange("(m p) -> m p", p=P)).then_inc(act_parm, 16)
                for d in range(2):
                    for gi, name in enumerate(("lru_w_a", "lru_w_i")):
                        src = lay(name, l)[d].rearrange("(k two) i j -> two i k j", two=2)
                        for half in range(2):
                            dst = BD[64 * half:64 * half + 64, 4 * d + 2 * gi:4 * d + 2 * gi + 2, 64 * half:64 * half + 64]
                            act.dma_start(dst, src[half]).then_inc(act_par, 16)
                            n += 1
                for dst, src in ((DTB, lay("ssd_dt_bias", l).rearrange("d h -> (d h)")),
                                 (ALOG, lay("ssd_a_log", l).rearrange("d h -> (d h)")),
                                 (DSK, lay("ssd_d", l)), (SSDN, lay("ssd_norm", l)), (SINK, lay("a_sink", l)),
                                 (RB, lay("router_bias", l))):
                    act.dma_start(dst, row_bcast(src)).then_inc(act_par, 16)
                    n += 1
                for name, h0, hn in (("d_q_norm", 0, 4), ("d_k_norm", 4, 2)):
                    for h in range(h0, h0 + hn):
                        act.dma_start(GQK[:, h, :], row_bcast(lay(name, l))).then_inc(act_par, 16)
                        n += 1
                act.dma_start(RW, lay("router_w", l).rearrange("(p c) e -> p c e", c=8)).then_inc(act_par, 16)
                n += 1
                assert n * 16 == PARAMS, n

                def heads_from(b, g, j):
                    act.activation(QKV[g][:, j, 0:256].rearrange("p (b a d) -> p a b d", a=2, b=2),
                                   b[:, 0:256].rearrange("p (a b d) -> p a b d", a=2, b=2), ACT.Copy)
                    act.activation(QKV[g][:, j, 256:512], b[:, 256:512], ACT.Copy).then_inc(a_pj, 1)

                for o in range(20):
                    act.wait_ge(pe_pj, o + 1)
                    b, j = bank[o % 4], o % 4
                    if o < 4:
                        act.activation(Z[:, j, :], b[:, 0:264], ACT.Copy).then_inc(a_pj, 1)
                    elif o < 6:
                        act.wait_ge(pool_clr, 7)
                        act.activation(LX[:, j, :, 2:258], b[:, :].rearrange("p (s n) -> p s n", s=2), ACT.Copy).then_inc(a_pj, 1)
                    elif o < 8:
                        act.activation(LG[:, j - 2, :], b[:, :], ACT.Gelu_apprx_tanh).then_inc(a_pj, 1)
                    elif o < 12:
                        act.activation(XBC[:, j, :, 2:258], b[:, :].rearrange("p (s n) -> p s n", s=2), ACT.Copy).then_inc(a_pj, 1)
                    elif o < 16:
                        heads_from(b, "A", j)
                    if o == 7:
                        act.wait_ge(act_par, PARAMS)
                        act.activation(EAL, ALOG, ACT.Exp).then_inc(a_al, 1)
                        act.wait_ge(v_v36, 1)
                        act.activation(E36, D36, ACT.Exp, scale=-1.0).then_inc(a_ex36, 1)
                    if o == 15:
                        for g in range(8):
                            d, gi, k = g // 4, (g // 2) % 2, g % 2
                            act.wait_ge(pe_lg, g + 1)
                            dst = (LR, LI)[gi][d][:, k, :]
                            col = 10 + 4 * gi + 2 * d + k
                            act.activation(dst, bank[4 + g % 4][:, :], ACT.Sigmoid, bias=PC[:, col:col + 1]).then_inc(a_lg, 1)
                        act.wait_ge(a_lg, 8)
                        act.wait_ge(v_c8, 1)
                        for d in range(2):
                            for k in range(2):
                                j2 = 2 * d + k
                                act.activation(LT[d][:, k, :], LR[d][:, k, :], ACT.Tanh, scale=C8[:, j2:j2 + 1]).then_inc(a_lt, 1)
                        act.wait_ge(a_lt, 4)
                        for d in range(2):
                            for k in range(2):
                                j2 = 2 * d + k
                                act.activation(LR[d][:, k, :], LR[d][:, k, :], ACT.Exp, scale=NC8[:, j2:j2 + 1]).then_inc(a_la, 1)
                        for k in range(4):
                            act.wait_ge(v_cv, k + 1)
                            act.activation(XC[:, k, :], XC[:, k, :], ACT.Silu, bias=PC[:, 38 + k:39 + k]).then_inc(a_xc, 1)
                        act.activation(Z[:, :, 0:256], Z[:, :, 0:256], ACT.Silu).then_inc(a_z, 1)
                    if o >= 16:
                        heads_from(b, "D", j)
                for d in range(2):
                    act.wait_ge(v_ld, d + 1)
                    act.activation(LT[d], LT[d], ACT.Sqrt).then_inc(a_lq, 1)
                act.wait_ge(v_cum, 1)
                act.activation(CT, CT, ACT.Exp).then_inc(a_cum, 1)
                for t in range(NT):
                    act.wait_ge(pe_xt, t + 1)
                    act.activation(XT[:, t, :], bank[5 + t % 2][:, 0:384], ACT.Copy).then_inc(a_xt, 1)
                act.wait_ge(v_qs, 1)
                act.activation(STT9, STT8, ACT.Sqrt, bias=EPSC, scale=1.0 / HD).then_inc(a_qn, 1)
                for t in range(NT):
                    for d in range(2):
                        act.wait_ge(pe_cb, 2 * t + d + 1)
                        if t == 0:
                            act.wait_ge(pe_st, 1)
                        else:
                            act.wait_ge(v_w, 2 * t - 1 + d)
                        for h in range(4):
                            j = t * 8 + d * 4 + h
                            ins = act.activation(ES[:, d, h, :], bank[4 + d][:, h * P:(h + 1) * P], ACT.Exp, bias=NCUM[:, j:j + 1])
                        ins.then_inc(a_e, 1)
                for t in range(NT):
                    act.wait_ge(v_yz, t + 1)
                    if t:
                        act.wait_ge(a_ssy, t)
                    act.activation(JUNK[:, 0:256], Z[:, t, 0:256], ACT.Square, accum_out=SS[:, t:t + 1]).then_inc(a_ssy, 1)
                act.wait_ge(a_ssy, 4)
                act.activation(SSTD, SS, ACT.Sqrt, bias=EPSC, scale=1.0 / 256).then_inc(a_ssy, 1)
                for k in range(2):
                    act.wait_ge(pe_ym, k + 1)
                    act.activation(MT[:, 2 + k, :], bank[2 + k][:, :], ACT.Copy).then_inc(a_ym, 1)
                act.wait_ge(v_lru, 1)
                for j in range(6):
                    act.wait_ge(pe_qk, j + 1)
                    act.activation(QT["AD"[j // 3]][:, j % 3, :], bank[4 + j % 4][:, :], ACT.Copy).then_inc(a_qk, 1)
                for u in range(NU + 2):
                    if u < NU:
                        g, t, h = units[u]
                        q = u % 3
                        nk = keys_of(t)
                        act.wait_ge(v_nm, u + 1)
                        if u >= 3:
                            act.wait_ge(pe_pt, u - 2)
                        act.activation(PB[q][:, 0:nk], bank[score_bank[q]][:, 0:nk], ACT.Exp, bias=SCOL[:, q, 1:2], scale=HD ** -0.5,
                                       accum_out=SCOL[:, q, 2:3]).then_inc(a_ex, 1)
                        if g == "A":
                            act.activation(SCOL[:, q, 3:4], SINK[:, h:h + 1], ACT.Exp, bias=SCOL[:, q, 1:2]).then_inc(a_es, 1)
                    if u >= 2:
                        w = u - 2
                        nk = keys_of(units[w][1])
                        act.wait_ge(pe_pt, w + 1)
                        if w >= 2:
                            act.wait_ge(pe_pv, w - 1)
                        act.activation(PTB[w % 2][:, 0:nk], bank[2 + w % 2][:, 0:nk], ACT.Copy).then_inc(a_pt, 1)
                for j in range(8):
                    act.wait_ge(pe_op, j + 1)
                    if j:
                        act.wait_ge(a_so, j)
                    act.activation(JUNK[:, 0:512], bank[j][:, :], ACT.Square, accum_out=S8[:, j:j + 1]).then_inc(a_so, 1)
                act.wait_ge(v_so, 1)
                act.activation(SSTD, SS, ACT.Sqrt, bias=EPSC, scale=1.0 / DM).then_inc(a_so, 1)
                norm_stats(5, True)
                out_of_transposes(8)
                act.wait_ge(pe_rt, 1)
                act.activation(SGT[0:64, :], bank[0][0:64, :], ACT.Sigmoid).then_inc(a_rt, 1)
                for k in range(2):
                    act.wait_ge(pe_sh, 2 * k + 1)
                    if k:
                        act.wait_ge(v_shm, k)
                    act.activation(SHS, bank[2 + 2 * k][:, :], ACT.Silu).then_inc(a_sh, 1)
                for j in range(8):
                    act.wait_ge(pe_sd, j + 1)
                    act.activation(YS[:, j // 2, (j % 2) * 512:(j % 2 + 1) * 512], bank[6 + j % 2][:, :], ACT.Copy).then_inc(a_sd, 1)
                act.sem_inc(a_y, 2)

                def xe(b_par, val):
                    act.wait_ge(pe_x, val)
                    act.activation(XGT[b_par], bank[(4, 6)[b_par]][:, :].rearrange("p (c h s) -> p c h s", c=4, h=2), ACT.Copy).then_inc(a_xe, 1)

                def silu(b_par, val, free):
                    act.wait_ge(pe_gu, val + 1)
                    if free is not None:
                        act.wait_ge(v_hid, free)
                    act.activation(HS[64:128, :], bank[b_par][0:64, 0:HID], ACT.Silu).then_inc(a_si, 1)

                act.wait_ge(v_tab, 1)
                pairs = act.value_load(NPR[0:1, 0:1], min_val=1, max_val=MAXB // 2 + 1)
                xe(0, 1)
                xe(1, 2)
                silu(0, 1, None)
                act.preload_act_table(ACT.Silu)
                with act.Fori(0, pairs) as i:
                    for u in range(2):
                        act.wait_ge(pe_h, i * 2 + (u + 1))
                        act.activation(HIDT[u], bank[5][:, 0:2 * SLOTS].rearrange("p (c s) -> p c s", c=2), ACT.Copy).then_inc(a_h, 1)
                        silu(1 - u, i * 2 + (u + 2), i * 2 + (u + 1))
                        xe(u, i * 2 + (u + 3))
                        act.wait_ge(pe_dn, i * 2 + (u + 2))
                        act.wait_ge(pool_s[u], i * 16 + 16)
                        act.activation(YSB[u], bank[2 + u][:, :], ACT.Copy).then_inc(a_y, 1)
                for t in range(NT):
                    act.wait_ge(v_yk, t + 1)
                    if t:
                        act.wait_ge(a_fs, t)
                    act.activation(H[:, 0, :], YS[:, t, :], ACT.Square, accum_out=SS[:, t:t + 1]).then_inc(a_fs, 1)
                act.wait_ge(a_fs, 4)
                act.activation(SSTD, SS, ACT.Sqrt, bias=EPSC, scale=1.0 / DM).then_inc(a_fs, 1)

            @block.tensor
            def _(pe):
                def transposes(base):
                    for j in range(8):
                        t, hh = j // 2, j % 2
                        pe.wait_ge(v_h, base // 2 + t + 1)
                        if base + j >= 2:
                            pe.wait_ge(a_tr, base + j - 1)
                        for q in range(4):
                            c = 4 * hh + q
                            src = H[:, t, c:DM:8] if base else H[:, t, c * P:(c + 1) * P]
                            ins = pe.transpose(bank[6 + j % 2][:, q * P:(q + 1) * P], src, IDENT)
                        ins.then_inc(pe_tr, 1)

                def ada_piece(i, b, width):
                    n = i if i < N_ADA1 else i + N_PROJ
                    pe.wait_ge(*landed(n))
                    w, q = at(ring[slot_of(n)], 8, width), width // 4
                    for c in range(8):
                        for j in range(4):
                            ins = pe.matmul(bank[b][32 * j:32 * j + 2, 0:q], SILC[:, c, :], w[:, c, q * j:q * j + q],
                                            start=(c == 0), stop=(c == 7))
                    ins.then_inc(pe_piece, 1)

                def ada2(i):
                    if i:
                        pe.wait_ge(v_ada, N_ADA1 + i)
                    ada_piece(N_ADA1 + i, 2, ada2_width[i])

                transposes(0)
                for n in range(N_ADA1):
                    if n >= 2:
                        pe.wait_ge(v_ada, n - 1)
                    ada_piece(n, n % 2, 512)
                pe.wait_ge(act_pr, 16 * 9)
                pe.transpose(bank[5][:, 0:66], PR[0:66, :], IDENT[0:66, 0:66]).then_inc(pe_pc, 1)
                pe.wait_ge(v_ada, N_ADA1)
                for n in range(N_ADA1):
                    ins = pe.transpose(bank[4][:, tile_of(n)], RAD1[:, n, :], IDENT)
                ins.then_inc(pe_m1, 1)
                pe.wait_ge(v_hm, 16)

                def project(n, kind, width):
                    pe.wait_ge(*landed(n))
                    w = at(ring[slot_of(n)], 8, width)
                    for j in range(4):
                        o = 4 * (n - P_PROJ) + j
                        if o >= 4:
                            pe.wait_ge(a_pj, o - 3)
                        for c in range(8):
                            if kind == "tokens":
                                ins = pe.matmul(bank[o % 4][:, 0:width], HT[:, c, tile_of(j)], w[:, c, :], start=(c == 0), stop=(c == 7))
                            else:
                                ins = pe.matmul(bank[o % 4][:, :], w[:, c, tile_of(j)], HT[:, c, :], start=(c == 0), stop=(c == 7))
                        ins.then_inc(pe_pj, 1)

                project(P_PROJ + 0, "tokens", 264)
                project(P_PROJ + 1, "channels", 512)
                project(P_PROJ + 2, "channels", 512)
                project(P_PROJ + 3, "tokens", 512)
                pe.wait_ge(v_u, 2)
                for g in range(8):
                    d, gi, k = g // 4, (g // 2) % 2, g % 2
                    if g >= 4:
                        pe.wait_ge(a_lg, g - 3)
                    pe.matmul(bank[4 + g % 4][:, :], BD[:, 4 * d + 2 * gi + k, :], U[:, k, :], start=True, stop=True).then_inc(pe_lg, 1)
                project(P_PROJ + 4, "tokens", 512)
                pe.wait_ge(v_aa, 1)
                pe.wait_ge(a_lg, 8)
                cu = bank[4][:, 0:32].rearrange("p (t e) -> p t e", e=8)
                pe.matmul(cu[:, :, 0:4], TRIU, AA[:, :, 0:4], start=True, stop=True)
                pe.matmul(cu[:, :, 4:8], TRIL, AA[:, :, 4:8], start=True, stop=True)
                pe.matmul(bank[4][:, 32:64], COLS[:, 3:4].broadcast_to([P, P]), AA.rearrange("p t e -> p (t e)"),
                          start=True, stop=True).then_inc(pe_cum, 1)
                pe.wait_ge(a_pj, 20)
                ada2(0)
                pe.wait_ge(a_xc, 4)
                for t in range(NT):
                    if t >= 2:
                        pe.wait_ge(a_xt, t - 1)
                    for k in range(3):
                        ins = pe.transpose(bank[5 + t % 2][:, k * P:(k + 1) * P], XC[:, k, tile_of(t)], IDENT)
                    ins.then_inc(pe_xt, 1)
                ada2(1)
                pe.wait_ge(v_xs, 2)
                for d in range(2):
                    for t in ((0, 1, 2), (1, 0, 3))[d]:
                        for g in range(2):
                            ins = pe.matmul(bank[6 + d][64 * g:64 * g + 64, tile_of(t)], XT[:, t, 256 + 64 * g:320 + 64 * g],
                                            XS[:, d, t, P * g:P * g + P], start=True, stop=True)
                ins.then_inc(pe_st, 1)
                pe.wait_ge(v_st, 1)
                pe.wait_ge(a_pj, 20)
                pe.wait_ge(v_cum, 1)
                for t in range(NT):
                    for d in range(2):
                        if t:
                            pe.wait_ge(a_e, 2 * t - 1 + d)
                        for h in range(4):
                            o = bank[4 + d][:, h * P:(h + 1) * P]
                            pe.matmul(o, AA[:, t, 4 * d + h:4 * d + h + 1].broadcast_to([P, P]), (TRIU, TRIL)[d], start=True, stop=False)
                            ins = pe.matmul(o, IDB, (NEGL, NEGU)[d], start=False, stop=True)
                        ins.then_inc(pe_cb, 1)
                    ada2(2 + t)
                    if t:
                        pe.wait_ge(v_w, 2 * t)
                    for g in range(2):
                        r = slice(64 * g, 64 * g + 64)
                        ins = pe.matmul(bank[(6, 3)[g]][:, 0:P], XC[r, 2, tile_of(t)], XC[r, 3, tile_of(t)], start=True, stop=True)
                    ins.then_inc(pe_gt, 1)
                    if t:
                        pe.wait_ge(v_y, t)
                    for d in range(2):
                        if (d, t) in ((0, 0), (1, 1)):
                            continue
                        for g in range(2):
                            r = slice(64 * g, 64 * g + 64)
                            ins = pe.matmul(bank[g][:, P * d:P * d + P], XC[r, 3, tile_of(t)], ST[r, d, t, :], start=True, stop=True)
                    ins.then_inc(pe_in, 1)
                    pe.wait_ge(v_w, 2 * t + 2)
                    for h in range(4):
                        for d in range(2):
                            ins = pe.matmul(bank[7][:, h * 64:h * 64 + 64], WS[:, d, h, :], XT[:, t, h * 64:h * 64 + 64],
                                            start=(d == 0), stop=(d == 1))
                    ins.then_inc(pe_y, 1)
                pe.wait_ge(v_yn, 4)
                pe.wait_ge(v_ada, N_ADA)
                for k in range(2):
                    for t in range(NT):
                        ins = pe.transpose(bank[2 + k][:, tile_of(t)], Z[:, t, P * k:P * k + P], IDENT)
                    ins.then_inc(pe_ym, 1)
                pe.wait_ge(v_y, 4)
                for j in range(6):
                    g, k = "AD"[j // 3], j % 3
                    pe.wait_ge(pool_rope, j // 3 + 1)
                    if j >= 4:
                        pe.wait_ge(a_qk, j - 3)
                    for t in range(NT):
                        ins = pe.transpose(bank[4 + j % 4][:, tile_of(t)], QKV[g][:, t, k * P:k * P + P], IDENT)
                    ins.then_inc(pe_qk, 1)
                pe.wait_ge(a_qk, 6)
                pe.wait_ge(a_ym, 2)

                def scores(u):
                    g, t, h = units[u]
                    nk = keys_of(t)
                    r = slice(64 * (h // 2), 64 * (h // 2) + 64)
                    if u >= 3:
                        pe.wait_ge(a_ex, u - 2)
                    sb = bank[score_bank[u % 3]]
                    masked = g == "A" and t >= 2
                    ins = pe.matmul(sb[:, 0:nk], QT[g][r, h % 2, tile_of(t)], QT[g][r, 2, 0:nk], start=True, stop=not masked)
                    if masked:
                        o = sb[:, 384:512] if t == 2 else sb[:, 256:384]
                        ins = pe.matmul(o, IDB, NEGU if t == 2 else NEGL, start=False, stop=True)
                    ins.then_inc(pe_s, 1)

                def turn(u):
                    nk = keys_of(units[u][1])
                    pe.wait_ge(v_p, u + 1)
                    if u >= 2:
                        pe.wait_ge(a_pt, u - 1)
                    for kb in range(nk // P):
                        ins = pe.transpose(bank[2 + u % 2][:, tile_of(kb)], PB[u % 3][:, tile_of(kb)], IDENT)
                    ins.then_inc(pe_pt, 1)

                def values(u):
                    g, t, h = units[u]
                    nk = keys_of(t)
                    pe.wait_ge(a_pt, u + 1)
                    if u // 4 >= 2 and h == 0:
                        pe.wait_ge(v_ot, u // 4 - 1)
                    o = bank[4 + (u // 4) % 2][64 * (h % 2):64 * (h % 2) + 64, (h // 2) * P:(h // 2 + 1) * P]
                    for kb in range(nk // P):
                        ins = pe.matmul(o, QKV[g][:, kb, 384 + 64 * (h // 2):448 + 64 * (h // 2)], PTB[u % 2][:, tile_of(kb)],
                                        start=(kb == 0), stop=(kb == nk // P - 1))
                    ins.then_inc(pe_pv, 1)

                scores(0)
                scores(1)
                for u in range(NU):
                    if u + 2 < NU:
                        scores(u + 2)
                    turn(u)
                    if u >= 1:
                        values(u - 1)
                values(NU - 1)
                pe.wait_ge(v_ot, 8)
                pe.wait_ge(v_lru, 1)
                pe.wait_ge(*landed(P_OUT))
                pe.wait_ge(*landed(P_OUT + 1))
                for t in range(NT):
                    for hf in range(2):
                        w = at(ring[slot_of(P_OUT + hf)], 8, 512)
                        for c in range(8):
                            ins = pe.matmul(bank[2 * t + hf][:, :], MT[:, c, tile_of(t)], w[:, c, :], start=(c == 0), stop=(c == 7))
                        ins.then_inc(pe_op, 1)
                transposes(8)
                pe.wait_ge(a_tr, 16)
                for c in range(8):
                    ins = pe.matmul(bank[0][0:64, :], RW[:, c, :], HT[:, c, :], start=(c == 0), stop=(c == 7))
                ins.then_inc(pe_rt, 1)
                pe.wait_ge(*landed(P_SH))
                w = at(ring[slot_of(P_SH)], 2, 8, HID)
                wd = at(ring[slot_of(P_SH)] + 4096, 2, DM)

                def shared_up(k, gu):
                    for c in range(8):
                        ins = pe.matmul(bank[2 + 2 * k + gu][:, :], w[:, gu, c, P * k:P * k + P], HT[:, c, :], start=(c == 0), stop=(c == 7))
                    ins.then_inc(pe_sh, 1)

                def shared_down(j):
                    t, hf = j // 2, j % 2
                    if j >= 2:
                        pe.wait_ge(a_sd, j - 1)
                    for k in range(2):
                        ins = pe.matmul(bank[6 + hf][:, :], SHT[:, k, tile_of(t)], wd[:, k, hf * 512:(hf + 1) * 512], start=(k == 0), stop=(k == 1))
                    ins.then_inc(pe_sd, 1)

                shared_up(0, 0)
                pe.wait_ge(a_rt, 1)
                for t in range(NT):
                    ins = pe.transpose(bank[1][:, 64 * t:64 * t + 64], SGT[0:64, tile_of(t)], IDENT[0:64, 0:64])
                ins.then_inc(pe_rtt, 1)
                shared_up(0, 1)
                shared_up(1, 0)
                shared_up(1, 1)
                pe.wait_ge(v_shm, 2)
                for j in range(8):
                    shared_down(j)
                pe.wait_ge(v_sel, 1)
                for t in range(NT):
                    for i2 in range(t + 1):
                        pe.matmul(bank[1][:, 64 * t:64 * t + 64], ONESB if i2 < t else TRISB, SELB[:, i2, :], start=(i2 == 0), stop=(i2 == t))
                for t in range(NT):
                    ins = pe.matmul(bank[1][:, 256:320], ONESB, SELB[:, t, :], start=(t == 0), stop=(t == NT - 1))
                ins.then_inc(pe_rk, 1)
                pe.wait_ge(v_eb, 1)
                pe.transpose(bank[0][0:1, 0:P], EB[:, 0:1], IDENT).then_inc(pe_row, 1)
                pe.sem_inc(pe_gu, 1)
                pe.sem_inc(pe_dn, 1)
                pe.wait_ge(v_tab, 1)
                pe.wait_ge(a_sd, 8)
                pairs = pe.value_load(NPR[0:1, 0:1], min_val=1, max_val=MAXB // 2 + 1)

                def expert_of(b):
                    return pe.value_load(TAB[0:1, bass.ds(b, 1)], min_val=0, max_val=NE - 1)

                def meta(b_par, b, val_oh, val_ix):
                    e = expert_of(b)
                    pe.wait_ge(v_oh, val_oh)
                    if val_ix is not None:
                        pe.wait_ge(v_ix, val_ix)
                    for t in range(NT):
                        ins = pe.matmul(bank[7][:, 0:3], OH[b_par][:, t, :], KV[:, t, bass.ds(e, 1), :].rearrange("p a c -> p (a c)"),
                                        start=(t == 0), stop=(t == NT - 1))
                    ins.then_inc(pe_meta, 1)

                def turn_tokens(b_par, val):
                    pe.wait_ge(pool_g[b_par], val)
                    for c in range(4):
                        ins = pe.transpose(bank[(4, 6)[b_par]][:, c * P:(c + 1) * P], XG[b_par][:, c:512:4], IDENT)
                    ins.then_inc(pe_x, 1)

                def up(b_par, k, chunks, last):
                    wv = at(ring[k], 2, 2, 4, HID)
                    for c8 in chunks:
                        hh, c = c8 // 4, c8 % 4
                        for gu in range(2):
                            ins = pe.matmul(bank[b_par][64 * gu:64 * gu + 64, 0:HID], XGT[b_par][:, c, hh, :], wv[:, gu, hh, c, :],
                                            start=(c8 == 0), stop=(c8 == 7))
                    if last:
                        ins.then_inc(pe_gu, 1)

                def expert_landed(e, k):
                    pe.wait_ge(sp_land[k], e * 16 + (base_land[k] + 48 - 16 * k))

                def down(b_par, k):
                    wv = at(ring[k] + 4096, 2, DM)
                    for c in range(2):
                        for cg in range(2):
                            ins = pe.matmul(bank[2 + b_par][64 * cg:64 * cg + 64, :], HIDT[b_par][:, c, :], wv[:, c, cg * 512:(cg + 1) * 512],
                                            start=(c == 0), stop=(c == 1))
                    ins.then_inc(pe_dn, 1)

                def turn_hidden():
                    for c in range(2):
                        ins = pe.transpose(bank[5][:, c * SLOTS:(c + 1) * SLOTS], HIDB[64:128, c:HID:2], IDENT[64:128, 64:128])
                    ins.then_inc(pe_h, 1)

                meta(0, 0, 1, None)
                meta(1, 1, 2, 1)
                turn_tokens(0, 16)
                meta(0, 2, 3, 2)
                turn_tokens(1, 16)
                e = expert_of(0)
                pe.wait_ge(a_xe, 1)
                for k in range(3):
                    with pe.If(e % 3 == k):
                        expert_landed(e, k)
                        up(0, k, range(8), True)
                with pe.Fori(0, pairs) as i:
                    for u in range(2):
                        b = i * 2 + u
                        meta(1 - u, b + 3, b + 4, b + 3)
                        if u == 0:
                            slot_now = pe.snap(expert_of(b) % 3)
                        else:
                            slot_now = slot
                        e = expert_of(b + 1)
                        slot = pe.snap(e % 3)
                        pe.wait_ge(a_xe, b + 2)
                        for k in range(3):
                            with pe.If(slot == k):
                                expert_landed(e, k)
                                up(1 - u, k, range(0, 5), False)
                                pe.wait_ge(v_hid, b + 1)
                                up(1 - u, k, range(5, 6), False)
                                turn_hidden()
                                up(1 - u, k, range(6, 8), True)
                        turn_tokens(u, i * 16 + 32)
                        pe.wait_ge(a_h, b + 1)
                        pe.wait_ge(a_y, b + 1)
                        for k in range(3):
                            with pe.If(slot_now == k):
                                down(u, k)

            @block.vector
            def _(dve):
                count = [0]

                def link(ins):
                    count[0] += 1
                    ins.then_inc(v_q, 1)
                    dve.wait_ge(v_q, count[0])

                def normed(base, mod_sem):
                    dve.wait_ge(a_ss, base)
                    link(dve.reciprocal(RSTD, SSTD))
                    dve.wait_ge(mod_sem, 32)
                    for t in range(NT):
                        s = t // 2
                        link(dve.scalar_tensor_tensor(out=H[:, t, :], in0=X[:, t, :], scalar=RSTD[:, t:t + 1], in1=MOD[:, 0, s, :],
                                                      op0=ALU.mult, op1=ALU.mult))
                        dve.tensor_tensor(H[:, t, :], H[:, t, :], MOD[:, 1, s, :], ALU.add).then_inc(v_h, 1)

                dve.wait_ge(a_ss, 5)
                link(dve.reciprocal(RSTD, SSTD))
                for t in range(NT):
                    dve.tensor_scalar(H[:, t, :], X[:, t, :], RSTD[:, t:t + 1], None, ALU.mult).then_inc(v_h, 1)

                def ada_rows(i):
                    dve.wait_ge(pe_piece, i + 1)
                    for j in range(4):
                        r = slice(32 * j, 32 * j + 2)
                        if i < N_ADA1:
                            ins = dve.tensor_copy(RAD1[r, i, :], bank[i % 2][r, 0:P])
                        else:
                            q, o = ada2_width[i - N_ADA1] // 4, 192 * (i - N_ADA1)
                            ins = dve.tensor_copy(RAD2[r, o:o + q], bank[2][r, 0:q])
                    ins.then_inc(v_ada, 1)

                dve.wait_ge(pool_clr, 1)
                for n in range(N_ADA1):
                    ada_rows(n)
                dve.wait_ge(pe_pc, 1)
                link(dve.tensor_copy(PC, bank[5][:, 0:66]))
                dve.wait_ge(pe_m1, 1)
                link(dve.tensor_tensor(MC, bank[4][:, :].rearrange("p (q r) -> p q r", r=32)[:, :, 0:2],
                                       PC[:, 42:58].unsqueeze(2).broadcast_to([P, 16, 2]), ALU.add))
                link(dve.scalar_tensor_tensor(out=MC[:, 8:16], in0=MC[:, 8:16], scalar=1.0,
                                              in1=PC[:, 58:66].unsqueeze(2).broadcast_to([P, 8, 2]), op0=ALU.add, op1=ALU.mult))
                dve.wait_ge(a_tr, 8)
                for c in range(8):
                    for s in range(2):
                        v = HT[:, c, s * CTX:(s + 1) * CTX]
                        dve.tensor_scalar(v, v, MC[:, 8 + c, s:s + 1], MC[:, c, s:s + 1], ALU.mult, ALU.add).then_inc(v_hm, 1)
                dve.tensor_scalar(V36[:, 32:36], PC[:, 18:22], -1.0, None, ALU.mult).then_inc(v_pcl, 1)
                dve.wait_ge(act_par, PARAMS)
                dve.tensor_scalar(NSINK, SINK, -1.0, None, ALU.mult).then_inc(v_pc, 1)
                dve.wait_ge(a_pj, 4)
                link(dve.tensor_tensor(V36[:, 0:32].rearrange("p (t e) -> p t e", e=8), Z[:, :, 256:264],
                                       DTB.unsqueeze(1).broadcast_to([P, NT, 8]), ALU.add))
                dve.wait_ge(v_pcl, 1)
                dve.scalar_tensor_tensor(out=D36, in0=V36, scalar=-1.0, in1=V36, op0=ALU.mult, op1=ALU.max).then_inc(v_v36, 1)

                def conv(dst, src, w0, step, bias):
                    d = dst.rearrange("p (s n) -> p s n", s=2)
                    if bias is None:
                        link(dve.tensor_scalar(d, src[:, :, 0:256], PC[:, w0:w0 + 1], None, ALU.mult))
                    else:
                        link(dve.tensor_scalar(d, src[:, :, 0:256], PC[:, w0:w0 + 1], bias, ALU.mult, ALU.add))
                    for j in range(1, 4):
                        ins = dve.scalar_tensor_tensor(out=d, in0=src[:, :, j:j + 256], scalar=PC[:, w0 + j * step:w0 + j * step + 1],
                                                       in1=d, op0=ALU.mult, op1=ALU.add)
                        if j < 3:
                            link(ins)
                    return ins

                for k in range(2):
                    dve.wait_ge(a_pj, 5 + k)
                    if k == 0:
                        dve.wait_ge(pe_tr, 8)
                    conv(U[:, k, :], LX[:, k], k, 2, PC[:, 8 + k:9 + k]).then_inc(v_u, 1)
                dve.wait_ge(a_ex36, 1)
                link(dve.tensor_scalar(D36, E36, 2.0, None, ALU.add))
                link(dve.reciprocal(D36, D36))
                link(dve.tensor_tensor(Z36, E36, D36, ALU.mult))
                link(dve.tensor_tensor(Q36, Z36, Z36, ALU.mult))
                link(dve.tensor_scalar(P36, Q36, 1.0 / 15, 1.0 / 13, ALU.mult, ALU.add))
                link(dve.tensor_tensor(P36, P36, Q36, ALU.mult))
                for m in (11, 9, 7, 5, 3):
                    link(dve.scalar_tensor_tensor(out=P36, in0=P36, scalar=1.0 / m, in1=Q36, op0=ALU.add, op1=ALU.mult))
                link(dve.scalar_tensor_tensor(out=P36, in0=P36, scalar=1.0, in1=Z36, op0=ALU.add, op1=ALU.mult))
                link(dve.tensor_scalar(V36, V36, 0.0, None, ALU.max))
                link(dve.scalar_tensor_tensor(out=P36, in0=P36, scalar=2.0, in1=V36, op0=ALU.mult, op1=ALU.add))
                DT = P36[:, 0:32].rearrange("p (t e) -> p t e", e=8)
                dve.wait_ge(a_al, 1)
                link(dve.tensor_scalar(C8, P36[:, 32:36], LRU_C, None, ALU.mult))
                dve.tensor_scalar(NC8, P36[:, 32:36], -LRU_C, None, ALU.mult).then_inc(v_c8, 1)
                dve.scalar_tensor_tensor(out=AA, in0=DT, scalar=-1.0, in1=EAL.unsqueeze(1).broadcast_to([P, NT, 8]),
                                         op0=ALU.mult, op1=ALU.mult).then_inc(v_aa, 1)
                dve.wait_ge(v_aa, 1)
                for k in range(4):
                    dve.wait_ge(a_pj, 9 + k)
                    conv(XC[:, k, :], XBC[:, k], 22 + k, 4, None).then_inc(v_cv, 1)
                for d in range(2):
                    dve.wait_ge(a_lt, 2 * d + 2)
                    link(dve.tensor_scalar(LD, LT[d], 1.0, None, ALU.add))
                    link(dve.reciprocal(LD, LD))
                    dve.scalar_tensor_tensor(out=LT[d], in0=LT[d], scalar=2.0, in1=LD, op0=ALU.mult, op1=ALU.mult).then_inc(v_ld, 1)
                    dve.wait_ge(v_ld, d + 1)
                for d in range(2):
                    link(dve.tensor_tensor(LI[d], LI[d], U, ALU.mult))
                    dve.wait_ge(a_lq, d + 1)
                    link(dve.tensor_tensor(LI[d], LI[d], LT[d], ALU.mult))
                dve.wait_ge(a_la, 4)
                for k in range(2):
                    link(dve.tensor_tensor_scan(LT[0][:, k, :], LR[0][:, k, :], LI[0][:, k, :], 0.0, ALU.mult, ALU.add))
                for k in range(2):
                    for s in range(2):
                        c = slice(s * 256, (s + 1) * 256)
                        o, a, x = (v[1][:, k, c][:, ::-1] for v in (LT, LR, LI))
                        link(dve.tensor_tensor_scan(o, a, x, 0.0 if s == 0 else LT[1][:, k, 0:1], ALU.mult, ALU.add))
                link(dve.tensor_tensor(LT[0], LT[0], LT[1], ALU.add))
                dve.wait_ge(pe_pj, 20)
                dve.tensor_tensor(MT[:, 4:6, :], LT[0], LG, ALU.mult).then_inc(v_lru, 1)
                dve.wait_ge(pe_cum, 1)
                link(dve.tensor_copy(CT[:, 0:32], bank[4][:, 0:32]))
                link(dve.tensor_copy(CT[:, 64:96], bank[4][:, 32:64]))
                link(dve.tensor_tensor(CT[:, 32:64], CT[:, 64:96], CT[:, 0:32], ALU.subtract))
                dve.tensor_scalar(NCUM, CT[:, 0:32], -1.0, None, ALU.mult).then_inc(v_cum, 1)
                ada_rows(N_ADA1)
                dve.wait_ge(a_cum, 1)
                ecum = CT[:, 0:32].rearrange("p (t d h) -> p t d h", t=NT, d=2)
                etot = CT[:, 64:96].rearrange("p (t d h) -> p t d h", t=NT, d=2)
                link(dve.tensor_tensor(TOE.rearrange("p t e -> p (t e)"), CT[:, 32:64], P36[:, 0:32], ALU.mult))
                link(dve.tensor_copy(DEC2[0:64], etot[0:64, :, :, 0:2]))
                link(dve.tensor_copy(DEC2[64:128], etot[64:128, :, :, 2:4]))
                dve.wait_ge(a_xt, 4)
                for d in range(2):
                    dve.tensor_tensor(XS[:, d].rearrange("p t (h n) -> p t h n", h=4),
                                      XT[:, :, 0:256].rearrange("p t (h n) -> p t h n", h=4),
                                      TOE[:, :, 4 * d:4 * d + 4].unsqueeze(3).broadcast_to([P, NT, 4, 64]), ALU.mult).then_inc(v_xs, 1)
                ada_rows(N_ADA1 + 1)
                dve.wait_ge(pool_sq, 1)
                dve.tensor_reduce(STT8, SQ.rearrange("p t (h d) -> p (t h) d", d=HD), AX, ALU.add).then_inc(v_qs, 1)
                dve.wait_ge(a_qn, 1)
                dve.reciprocal(STT8, STT9).then_inc(v_qr, 1)
                dve.wait_ge(pe_st, 1)
                for d, order in enumerate(((0, 1, 2, 3), (1, 0, 3, 2))):
                    link(dve.tensor_copy(ST[:, d, order[1], :], bank[6 + d][:, tile_of(order[0])]))
                    for k in (1, 2):
                        t, n = order[k], order[k + 1]
                        tmp = YT[0][:, 0:P].rearrange("p (h n) -> p h n", h=2)
                        link(dve.tensor_tensor(tmp, ST[:, d, t, :].rearrange("p (h n) -> p h n", h=2),
                                               DEC2[:, t, d, :].unsqueeze(2).broadcast_to([P, 2, 64]), ALU.mult))
                        ins = dve.tensor_tensor(ST[:, d, n, :], YT[0][:, 0:P], bank[6 + d][:, tile_of(t)], ALU.add)
                        if (d, k) == (1, 2):
                            ins.then_inc(v_st, 1)
                            dve.wait_ge(v_st, 1)
                        else:
                            link(ins)
                dve.wait_ge(a_z, 1)
                for t in range(NT):
                    for d in range(2):
                        dve.wait_ge(a_e, 2 * t + d + 1)
                        if d == 0:
                            dve.wait_ge(pe_gt, t + 1)
                            if t:
                                dve.wait_ge(pe_y, t)
                        for h in range(4):
                            j = t * 8 + 4 * d + h
                            ins = dve.scalar_tensor_tensor(out=WS[:, d, h, :], in0=ES[:, d, h, :], scalar=P36[:, j:j + 1],
                                                           in1=bank[(6, 3)[h // 2]][:, 0:P], op0=ALU.mult, op1=ALU.mult)
                        ins.then_inc(v_w, 1)
                    ada_rows(N_ADA1 + 2 + t)
                    h4 = lambda v: v.rearrange("p (h n) -> p h n", h=4)
                    dve.wait_ge(pe_in, t + 1)
                    dirs = [d for d in range(2) if (d, t) not in ((0, 0), (1, 1))]
                    ds = slice(dirs[0], dirs[-1] + 1)
                    for g in range(2):
                        link(dve.tensor_tensor(YTD[:, ds, 2 * g:2 * g + 2, :],
                                               bank[g][:, 0:256].rearrange("p (d h n) -> p d h n", d=2, h=2)[:, ds],
                                               ecum[:, t, ds, 2 * g:2 * g + 2].unsqueeze(3).broadcast_to([P, len(dirs), 2, 64]), ALU.mult))
                    link(dve.tensor_tensor(h4(YT[0]), h4(XT[:, t, 0:256]), DSK.unsqueeze(2).broadcast_to([P, 4, 64]), ALU.mult))
                    dve.wait_ge(pe_y, t + 1)
                    dve.tensor_tensor(YT[0], YT[0], bank[7][:, 0:256], ALU.add).then_inc(v_y, 1)
                    dve.wait_ge(v_y, t + 1)
                    for d in dirs:
                        link(dve.tensor_tensor(YT[0], YT[0], YT[1 + d], ALU.add))
                    dve.tensor_tensor(Z[:, t, 0:256], Z[:, t, 0:256], YT[0], ALU.mult).then_inc(v_yz, 1)
                dve.wait_ge(v_yz, 4)
                dve.wait_ge(a_ssy, 5)
                link(dve.reciprocal(RSTD, SSTD))
                for t in range(NT):
                    dve.scalar_tensor_tensor(out=Z[:, t, 0:256], in0=Z[:, t, 0:256], scalar=RSTD[:, t:t + 1], in1=SSDN,
                                             op0=ALU.mult, op1=ALU.mult).then_inc(v_yn, 1)

                def bound(u):
                    g, t, h = units[u]
                    q = u % 3
                    dve.wait_ge(pe_s, u + 1)
                    link(dve.tensor_reduce(SCOL[:, q, 0:1], bank[score_bank[q]][:, 0:keys_of(t)], AX, ALU.max))
                    if g == "A":
                        dve.tensor_scalar(SCOL[:, q, 1:2], SCOL[:, q, 0:1], -HD ** -0.5, NSINK[:, h:h + 1], ALU.mult, ALU.min).then_inc(v_nm, 1)
                    else:
                        dve.tensor_scalar(SCOL[:, q, 1:2], SCOL[:, q, 0:1], -HD ** -0.5, None, ALU.mult).then_inc(v_nm, 1)

                def scaled(u):
                    g, t, h = units[u]
                    q = u % 3
                    nk = keys_of(t)
                    dve.wait_ge(a_ex, u + 1)
                    if g == "A":
                        dve.wait_ge(a_es, u + 1)
                        link(dve.tensor_tensor(SCOL[:, q, 2:3], SCOL[:, q, 2:3], SCOL[:, q, 3:4], ALU.add))
                    link(dve.reciprocal(MX[:, q, 0:1], SCOL[:, q, 2:3]))
                    dve.tensor_scalar(PB[q][:, 0:nk], PB[q][:, 0:nk], MX[:, q, 0:1], None, ALU.mult).then_inc(v_p, 1)

                def heads_out(j):
                    g, t, _h = units[4 * j]
                    c0 = 0 if g == "A" else 6
                    dve.wait_ge(pe_pv, 4 * j + 4)
                    dve.tensor_copy(MT[:, c0:c0 + 2, tile_of(t)], bank[4 + j % 2][:, 0:256].rearrange("p (c n) -> p c n", c=2)).then_inc(v_ot, 1)

                bound(0)
                bound(1)
                for u in range(NU):
                    scaled(u)
                    if u + 2 < NU:
                        bound(u + 2)
                    if u == 8:
                        dve.wait_ge(pool_m64, 16)
                        dve.wait_ge(act_parm, 128)
                        link(dve.tensor_tensor(M64[0:64, :], M64[0:64, :], B64[0:64, :], ALU.add))
                        dve.scalar_tensor_tensor(out=M64[0:64, :], in0=M64[0:64, :], scalar=COLS[0:64, 9:10], in1=G64[0:64, :],
                                                 op0=ALU.add, op1=ALU.mult).then_inc(v_m64, 1)
                    if u >= 5 and u % 4 == 1:
                        heads_out(u // 4 - 1)
                heads_out(NU // 4 - 1)
                dve.wait_ge(a_so, 8)
                s8 = S8.rearrange("p (t h) -> p t h", h=2)
                dve.tensor_tensor(SS, s8[:, :, 0], s8[:, :, 1], ALU.add).then_inc(v_so, 1)
                dve.wait_ge(a_so, 9)
                link(dve.reciprocal(RSTD, SSTD))
                dve.wait_ge(pool_gate1, 16)
                for t in range(NT):
                    for hf in range(2):
                        c = slice(hf * 512, (hf + 1) * 512)
                        link(dve.scalar_tensor_tensor(out=OTMP[hf], in0=bank[2 * t + hf][:, :], scalar=RSTD[:, t:t + 1],
                                                      in1=MOD[:, 2, t // 2, c], op0=ALU.mult, op1=ALU.mult))
                        ins = dve.tensor_tensor(X[:, t, c], X[:, t, c], OTMP[hf], ALU.add)
                    ins.then_inc(v_x, 1)
                normed(10, pool_mod2)
                dve.memset(GS12, 1.0e30).then_inc(v_pcl, 1)
                dve.memset(ONES64, 1.0).then_inc(v_pcl, 1)
                dve.memset(KV[:, :, :, 0], 0.0).then_inc(v_pcl, 1)
                dve.memset(BASE, 0.0).then_inc(v_pcl, 1)
                dve.memset(TAB, NE - 1).then_inc(v_pcl, 1)
                dve.wait_ge(v_pcl, 6)
                link(dve.tensor_scalar(KV[:, :, :, 0], KV[:, :, :, 0], COLS[:, 0:1], None, ALU.add))
                for t in range(NT):
                    link(dve.memset(KV[:, t, :, 1], float(P * t)))
                dve.wait_ge(pe_rtt, 1)
                dve.tensor_copy(SC, bank[1][:, 0:256].rearrange("p (t e) -> p t e", t=NT)).then_inc(v_sc, 1)
                dve.wait_ge(v_sc, 1)
                link(dve.tensor_tensor(BI, SC, RB.unsqueeze(1).broadcast_to([P, NT, NE]), ALU.add))
                for t in range(NT):
                    for g in range(NG):
                        ins = dve.max(TOP[:, t, g, :], BI[:, t, 8 * g:8 * g + 8])
                link(ins)
                link(dve.tensor_tensor(GS12[:, :, 0:8], TOP[:, :, :, 0], TOP[:, :, :, 1], ALU.add))
                for t in range(NT):
                    ins = dve.max(M8[:, t, :], GS12[:, t, :])
                link(ins)
                for t in range(NT):
                    ins = dve.match_replace(GR[:, t, :], M8[:, t, :], GS12[:, t, :], MARK)
                link(ins)
                link(dve.tensor_scalar(GR[:, :, 0:8], GR[:, :, 0:8], MARK, NEG, ALU.not_equal, ALU.mult))
                link(dve.tensor_tensor(BI.rearrange("p t (g e) -> p t g e", g=NG), BI.rearrange("p t (g e) -> p t g e", g=NG),
                                       GR[:, :, 0:8].unsqueeze(3).broadcast_to([P, NT, NG, 8]), ALU.add))
                for t in range(NT):
                    ins = dve.max(M8[:, t, :], BI[:, t, :])
                link(ins)
                for t in range(NT):
                    ins = dve.match_replace(MR[:, t, :], M8[:, t, :], BI[:, t, :], MARK)
                link(ins)
                link(dve.tensor_scalar(SEL, MR, MARK, None, ALU.is_equal))
                link(dve.tensor_tensor(SC, SC, SEL, ALU.mult))
                link(dve.tensor_tensor(SEL, SEL, CM.unsqueeze(2).broadcast_to([P, NT, NE]), ALU.mult))
                dve.tensor_copy(SELB, SEL).then_inc(v_sel, 1)
                for k in range(2):
                    dve.wait_ge(a_sh, k + 1)
                    dve.wait_ge(pe_sh, 2 * k + 2)
                    dve.tensor_tensor(SHT[:, k, :], SHS, bank[3 + 2 * k][:, :], ALU.mult).then_inc(v_shm, 1)
                for t in range(NT):
                    ins = dve.tensor_tensor_scan(CI[:, t, :], ONES64, SEL[:, t, :], 0.0, ALU.mult, ALU.add)
                link(ins)
                link(dve.tensor_scalar(KV[:, :, :, 2], CI, -1.0, float(T), ALU.add, ALU.mult))
                dve.wait_ge(pe_rk, 1)
                link(dve.tensor_copy(CNT, bank[1][:, 256:320]))
                link(dve.tensor_scalar(NB, CNT, 0.0, None, ALU.is_gt))
                for m in range(1, T // SLOTS):
                    link(dve.scalar_tensor_tensor(out=NB, in0=CNT, scalar=float(m * SLOTS), in1=NB, op0=ALU.is_gt, op1=ALU.add))
                link(dve.tensor_tensor_scan(PEND, ONES64, NB, 0.0, ALU.mult, ALU.add))
                link(dve.tensor_tensor(PST, PEND, NB, ALU.subtract))
                link(dve.tensor_scalar(LE, PEND, COLS[:, 1:2], None, ALU.is_le))
                link(dve.tensor_reduce(EB[:, 1:2], LE, AX, ALU.add))
                dve.tensor_scalar(EB[:, 0:1], EB[:, 1:2], float(NE - 1), None, ALU.min).then_inc(v_eb, 1)
                link(dve.scalar_tensor_tensor(out=GG, in0=PST.unsqueeze(1).broadcast_to([P, NT, NE]), scalar=float(SLOTS),
                                              in1=bank[1][:, 0:256].rearrange("p (t e) -> p t e", t=NT), op0=ALU.mult, op1=ALU.add))
                link(dve.scalar_tensor_tensor(out=GG, in0=GG, scalar=1.0, in1=SEL, op0=ALU.add, op1=ALU.mult))
                link(dve.tensor_scalar(GG, GG, -1.0, None, ALU.add))
                link(dve.tensor_copy(TABP, PEND[0:1, :]))
                link(dve.tensor_scalar(NBH[0:1, :], PEND[0:1, NE - 1:NE], 0.5, 0.25, ALU.mult, ALU.add))
                link(dve.tensor_copy(NPR, NBH[0:1, :]))
                dve.wait_ge(pe_row, 1)
                dve.tensor_copy(TAB[0:1, 0:P], bank[0][0:1, 0:P]).then_inc(v_tab, 1)
                dve.wait_ge(v_tab, 1)

                def expert_of(b):
                    return dve.value_load(TAB[0:1, bass.ds(b, 1)], min_val=0, max_val=NE - 1)

                def one_hot(par, b, chain):
                    e = expert_of(b)
                    if not (isinstance(b, int) and b == 0):
                        dve.wait_ge(v_oh, b)
                    chain(dve.tensor_scalar(RR.unsqueeze(2), GG[:, :, bass.ds(e, 1)], BASE[:, 0:1], None, ALU.subtract))
                    chain(dve.tensor_scalar(BASE, BASE, float(SLOTS), None, ALU.add))
                    dve.tensor_tensor(OH[par], IOTA.unsqueeze(1).broadcast_to([P, NT, P]),
                                      RR.unsqueeze(2).broadcast_to([P, NT, P]), ALU.is_equal).then_inc(v_oh, 1)

                def rows(par, b, six, chain):
                    if not (isinstance(b, int) and b == 0):
                        dve.wait_ge(v_ix, b)
                    chain(dve.tensor_copy(M3[:, 0:3], bank[7][:, 0:3]))
                    chain(dve.tensor_scalar(TK[:, 0:1], M3[:, 0:1], 0.0, BIG_ROW, ALU.is_equal, ALU.mult))
                    chain(dve.scalar_tensor_tensor(out=TK[:, 1:2], in0=M3[:, 0:1], scalar=M3[:, 1:2], in1=TK[:, 0:1], op0=ALU.add, op1=ALU.add))
                    chain(dve.tensor_scalar(GIX[par], TK[:, 1:2], 2.0, COLS[:, 2:3], ALU.mult, ALU.add))
                    chain(dve.tensor_tensor(TK[:, 2:3], TK[:, 1:2], M3[:, 2:3], ALU.add))
                    dve.tensor_scalar(six, TK[:, 2:3], 2.0, COLS[:, 2:3], ALU.mult, ALU.add).then_inc(v_ix, 1)

                one_hot(0, 0, link)
                one_hot(1, 1, link)
                for b in range(3):
                    dve.wait_ge(pe_meta, b + 1)
                    if b == 2:
                        dve.wait_ge(pool_g[0], 16)
                    rows(b % 2, b, SIXT[:, b:b + 1], link)
                    if b < 2:
                        one_hot(b % 2, b + 2, link)
                link(dve.tensor_reduce(WSUM, SC, AX, ALU.add))
                link(dve.reciprocal(WSUM, WSUM))
                link(dve.tensor_scalar(WSUM, WSUM, ROUTED_SCALE, None, ALU.mult))
                link(dve.tensor_tensor(SC, SC, WSUM.unsqueeze(2).broadcast_to([P, NT, NE]), ALU.mult))
                for t in range(NT):
                    for k in range(TOPK):
                        link(dve.scalar_tensor_tensor(out=LE, in0=CI[:, t, :], scalar=float(k + 1), in1=SC[:, t, :],
                                                      op0=ALU.is_equal, op1=ALU.mult, accum_out=WK[:, t, k:k + 1]))

                def product(par, val, hfree):
                    dve.wait_ge(a_si, val)
                    if hfree is not None:
                        dve.wait_ge(pe_h, hfree)
                    dve.tensor_tensor(HIDB[64:128, :], HS[64:128, :], bank[par][64:128, 0:HID], ALU.mult).then_inc(v_hid, 1)

                product(0, 1, None)
                pairs = dve.value_load(NPR[0:1, 0:1], min_val=1, max_val=MAXB // 2 + 1)
                PER = 7
                with dve.Fori(0, pairs) as i:
                    for u in range(2):
                        b = i * 2 + u
                        n = [0]

                        def chain(ins):
                            n[0] += 1
                            ins.then_inc(v_ml, 1)
                            dve.wait_ge(v_ml, b * PER + n[0])

                        dve.wait_ge(pe_meta, b + 4)
                        dve.wait_ge(pool_g[1 - u], i * 16 + 16 * (1 + u))
                        rows(1 - u, b + 3, SIXT[:, bass.ds(b + 3, 1)], chain)
                        one_hot(u, b + 4, chain)
                        product(1 - u, b + 2, b + 1)
                        dve.wait_ge(pool_s[u], i * 16 + 16)
                        dve.tensor_copy(SIXS[u], SIXT[:, bass.ds(b, 1)]).then_inc(v_six, 1)
                        assert n[0] == PER, n[0]
                for t in range(NT):
                    dve.wait_ge(sp_yk[t % 2], 16 * (t // 2 + 1))
                    if t == 0:
                        dve.wait_ge(a_sd, 8)
                    for k in range(TOPK):
                        ins = dve.scalar_tensor_tensor(out=YS[:, t, :], in0=YK[t % 2][:, k, :], scalar=WK[:, t, k:k + 1],
                                                       in1=YS[:, t, :], op0=ALU.mult, op1=ALU.add)
                        if k < TOPK - 1:
                            link(ins)
                    ins.then_inc(v_yk, 1)
                dve.wait_ge(a_fs, 5)
                link(dve.reciprocal(RSTD, SSTD))
                dve.wait_ge(pool_gate2, 16)
                for t in range(NT):
                    link(dve.scalar_tensor_tensor(out=YS[:, t, :], in0=YS[:, t, :], scalar=RSTD[:, t:t + 1], in1=MOD[:, 2, t // 2, :],
                                                  op0=ALU.mult, op1=ALU.mult))
                    dve.tensor_tensor(X[:, t, :], X[:, t, :], YS[:, t, :], ALU.add).then_inc(v_end, 1)
                dve.memset(CM[:, 0:2], 0.0).then_inc(v_end, 1)
                dve.wait_ge(v_end, 5)
          nc.all_engine_barrier(sems_to_clear=all_sems)

        with nc.Block() as block:
            @block.sync
            def _(sp):
                for t in range(2):
                    sp.dma_start(out[0, t * P:(t + 1) * P, :], X[:, 2 + t, :]).then_inc(sp_land[0], 16)
                sp.wait_ge(sp_land[0], 32)


def host_constants():
    import numpy as np
    p = np.arange(P)[:, None]
    f = np.arange(P)[None, :]
    c = np.zeros((P, CW), np.float32)

    def put(name, v):
        c[:, COFF[name]:COFF[name] + v.shape[1]] = v

    put("ident", (p == f).astype(np.float32))
    put("triU", (p <= f).astype(np.float32))
    put("triL", (p >= f).astype(np.float32))
    put("iota", np.broadcast_to(f % SLOTS, (P, P)).astype(np.float32))
    put("triS", (p < f).astype(np.float32))
    put("negL", np.where(p > f, np.float32(NEG), np.float32(0)))
    put("negU", np.where(f > p, np.float32(NEG), np.float32(0)))
    pos = np.arange(SEQ)
    inv = np.float32(10000.0) ** (-np.arange(0, HD // 2, 2, dtype=np.float32) / np.float32(HD // 2))
    ang = np.concatenate([(pos // 64).astype(np.float32)[:, None] * inv, (pos % 64).astype(np.float32)[:, None] * inv], axis=-1)
    for name, v in (("cos", np.cos(ang)), ("sin", np.sin(ang))):
        put(name, v.astype(np.float32).reshape(2, P, 32).transpose(1, 0, 2).reshape(P, 64))
    cols = np.zeros((P, 16), np.float32)
    pp = np.arange(P)
    cols[:, 0] = pp + 1
    cols[:, 1] = pp
    cols[:, 2] = pp >= 64
    cols[:, 3] = 1.0
    cols[:, 4] = EPS
    cols[:, 9] = (pp % 32) // 8 == 2
    put("cols", cols)
    return c


PARAMS = 16 * (8 + 6 + 6 + 1)
_INS = ["x", "c", "ctx", "c_ctx", "w_ada", "b_ada", "g_mix_pre", "g_mix_post", "g_ffn_pre", "g_ffn_post", "w_in", "w_out",
        "a_sink", "ssd_conv_w", "ssd_conv_b", "ssd_dt_bias", "ssd_a_log", "ssd_d", "ssd_norm",
        "lru_conv_w", "lru_conv_b", "lru_w_a", "lru_b_a", "lru_w_i", "lru_b_i", "lru_lambda",
        "d_q_norm", "d_k_norm", "router_w", "router_bias", "exp_w_gate", "exp_w_up", "exp_w_down",
        "sh_w_gate", "sh_w_up", "sh_w_down"]


def kernel(**inputs):
    import numpy as np
    import concourse.bacc as bacc
    from concourse.bass_utils import run_bass_kernel_spmd

    nc = bacc.Bacc("TRN2", target_bir_lowering=False, num_devices=1)
    arrays = {f"in_{n}": np.ascontiguousarray(inputs[n]) for n in _INS}
    arrays["in_consts"] = host_constants()
    aps = {n[3:]: nc.dram_tensor(n, a.shape, F32, kind="ExternalInput").ap() for n, a in arrays.items()}
    out = nc.dram_tensor("out", (1, SEQ, DM), F32, kind="ExternalOutput").ap()
    build(nc, aps, out)
    r = run_bass_kernel_spmd(nc, [arrays], core_ids=[0])
    return r.results[0]["out"]
```
